# Optimizing a Trainium2 kernel written in Bass

```python
import jax, jax.numpy as jnp
from jax import lax
import numpy as np

D_MODEL = 1024
BATCH = 1
SEQ = 1024
DEPTH = 2

CTX_LEN = 256
GRID_W = 64
HGRN_HEADS = 8
HGRN_HEAD_DIM = D_MODEL // HGRN_HEADS
CHUNK = 64
CONV_WIDTH = 3
FFN_HIDDEN = ((8 * D_MODEL + 3 * 256 - 1) // (3 * 256)) * 256
N_HGRN_LAYERS = (DEPTH + 1) // 2
N_CONV_LAYERS = DEPTH // 2
N_MOD = 6
EPS = 1e-6
F_FLOOR = 1e-6

kernel_name = "hybrid_hgrn2_shortconv_dit_trunk"

def _rmsnorm(x, w):
    xf = x.astype(jnp.float32)
    y = xf * lax.rsqrt(jnp.mean(xf * xf, axis=-1, keepdims=True) + EPS)
    return (y * w.astype(jnp.float32)).astype(x.dtype)

def _modulate(h, shift, scale):
    return h * (1 + scale) + shift

def _heads(t):
    return t.reshape(t.shape[:-1] + (HGRN_HEADS, HGRN_HEAD_DIM))

def _chunk_scan(q, k, v, log_f, s0):
    b, l, h, _ = q.shape
    dv = v.shape[-1]
    n = l // CHUNK

    def to_chunks(t):
        return t.astype(jnp.float32).reshape(b, n, CHUNK, h, t.shape[-1]).transpose(1, 0, 3, 2, 4)

    mask = jnp.tril(jnp.ones((CHUNK, CHUNK), dtype=bool))[:, :, None]

    def step(s, inp):
        qc, kc, vc, gc = inp
        cum = jnp.cumsum(gc, axis=2)
        o_inter = jnp.einsum("bhtk,bhkv->bhtv", qc * jnp.exp(cum), s)
        diff = cum[:, :, :, None, :] - cum[:, :, None, :, :]
        decay = jnp.where(mask, jnp.exp(jnp.where(mask, diff, 0.0)), 0.0)
        scores = jnp.einsum("bhtk,bhsk,bhtsk->bhts", qc, kc, decay)
        o = o_inter + jnp.einsum("bhts,bhsv->bhtv", scores, vc)
        last = cum[:, :, -1:, :]
        s_new = jnp.exp(last[:, :, 0, :])[..., None] * s + jnp.einsum(
            "bhsk,bhsv->bhkv", kc * jnp.exp(last - cum), vc)
        return s_new, o

    s_fin, o = lax.scan(step, s0, (to_chunks(q), to_chunks(k), to_chunks(v), to_chunks(log_f)))
    return o.transpose(1, 0, 3, 2, 4).reshape(b, l, h, dv), s_fin

def _forget_gates(z, lb):
    zf = z.astype(jnp.float32)
    f = lb + (1.0 - lb) * jax.nn.sigmoid(zf)
    log_f = jnp.log(jnp.maximum(f, F_FLOOR))
    k = (1.0 - lb) * jax.nn.sigmoid(-zf)
    return _heads(k), _heads(log_f)

def _direction(qc, vc, zc, ql, vl, zl, lb, s0):
    kc, lc = _forget_gates(zc, lb)
    kl, ll = _forget_gates(zl, lb)
    oc, s_ctx = _chunk_scan(qc, kc, vc, lc, s0)
    ol, _ = _chunk_scan(ql, kl, vl, ll, s_ctx)
    return oc, ol

def _readout(o, g, g_norm, w_out, dtype):
    o = o * lax.rsqrt(jnp.mean(o * o, axis=-1, keepdims=True) + EPS) * g_norm.astype(jnp.float32)
    o = o * jax.nn.silu(_heads(g.astype(jnp.float32)))
    return o.reshape(o.shape[:-2] + (HGRN_HEADS * HGRN_HEAD_DIM,)).astype(dtype) @ w_out

def _hgrn2_mixer(h, hc, w_in, w_out, g_norm, lb, need_ctx_out):
    lb = lb.astype(jnp.float32)
    q_scale = HGRN_HEAD_DIM ** -0.5
    ql, vl, zfl, zbl, gl = jnp.split(h @ w_in, 5, axis=-1)
    qc, vc, zfc, zbc, gc = jnp.split(hc @ w_in, 5, axis=-1)
    ql, qc = _heads(ql) * q_scale, _heads(qc) * q_scale
    vl, vc = _heads(vl), _heads(vc)
    s0 = jnp.zeros((h.shape[0], HGRN_HEADS, HGRN_HEAD_DIM, HGRN_HEAD_DIM), jnp.float32)

    def flip(t):
        return jnp.flip(t, axis=1)

    oc_f, ol_f = _direction(qc, vc, zfc, ql, vl, zfl, lb, s0)
    oc_b, ol_b = _direction(flip(qc), flip(vc), flip(zbc), flip(ql), flip(vl), flip(zbl), lb, s0)
    y = _readout(ol_f + flip(ol_b), gl, g_norm, w_out, h.dtype)
    yc = _readout(oc_f + flip(oc_b), gc, g_norm, w_out, hc.dtype) if need_ctx_out else None
    return y, yc

def _dwconv(u, w):
    pad = CONV_WIDTH // 2
    length = u.shape[1]
    up = jnp.pad(u, ((0, 0), (pad, CONV_WIDTH - 1 - pad), (0, 0)))
    out = up[:, 0:length] * w[0]
    for j in range(1, CONV_WIDTH):
        out = out + up[:, j:j + length] * w[j]
    return out

def _short_conv_mixer(h, w_in, w_conv, w_out, rows):
    b, l, d = h.shape
    gate_b, gate_c, xin = jnp.split(h @ w_in, 3, axis=-1)
    u = gate_c * xin
    if rows is None:
        y = _dwconv(u, w_conv)
    else:
        y = _dwconv(u.reshape(b * rows, GRID_W, d), w_conv).reshape(b, l, d)
    return (gate_b * y) @ w_out

def _swiglu(h, w_in, w_out):
    gate, up = jnp.split(h @ w_in, 2, axis=-1)
    return (jax.nn.silu(gate) * up) @ w_out

def setup_inputs(seed: int = 0) -> dict:
    key = jax.random.key(seed)
    ks = jax.random.split(key, 16)
    d = D_MODEL

    def nrm(k, shape, scale):
        return scale * jax.random.normal(k, shape, jnp.float32)

    return {
        "x": nrm(ks[0], (BATCH, SEQ, d), 1.0),
        "c": nrm(ks[1], (BATCH, d), 1.0),
        "ctx": nrm(ks[2], (BATCH, CTX_LEN, d), 1.0),
        "c_ctx": nrm(ks[3], (d,), 1.0),
        "ada_w": nrm(ks[4], (DEPTH, d, N_MOD * d), 0.5 * d ** -0.5),
        "ada_b": nrm(ks[5], (DEPTH, N_MOD * d), 0.01),
        "norm_w": 1.0 + nrm(ks[6], (DEPTH, 4, d), 0.05),
        "hgrn_w_in": nrm(ks[7], (N_HGRN_LAYERS, d, 5 * d), d ** -0.5),
        "hgrn_w_out": nrm(ks[8], (N_HGRN_LAYERS, d, d), d ** -0.5),
        "hgrn_gnorm": 1.0 + nrm(ks[9], (N_HGRN_LAYERS, HGRN_HEAD_DIM), 0.05),
        "hgrn_lb": 1.0 + nrm(ks[10], (N_HGRN_LAYERS, HGRN_HEADS * HGRN_HEAD_DIM), 0.5),
        "conv_w_in": nrm(ks[11], (N_CONV_LAYERS, d, 3 * d), d ** -0.5),
        "conv_w": nrm(ks[12], (N_CONV_LAYERS, CONV_WIDTH, d), CONV_WIDTH ** -0.5),
        "conv_w_out": nrm(ks[13], (N_CONV_LAYERS, d, d), d ** -0.5),
        "ffn_w_in": nrm(ks[14], (DEPTH, d, 2 * FFN_HIDDEN), d ** -0.5),
        "ffn_w_out": nrm(ks[15], (DEPTH, FFN_HIDDEN, d), FFN_HIDDEN ** -0.5),
    }

def reference(x, c, ctx, c_ctx, ada_w, ada_b, norm_w, hgrn_w_in, hgrn_w_out, hgrn_gnorm, hgrn_lb,
              conv_w_in, conv_w, conv_w_out, ffn_w_in, ffn_w_out):
    rows = x.shape[1] // GRID_W
    soft = jax.nn.softmax(hgrn_lb.astype(jnp.float32), axis=0)
    lower_bounds = jnp.cumsum(soft, axis=0) - soft[0]
    silu_c = jax.nn.silu(c)
    silu_cc = jax.nn.silu(c_ctx)
    for l in range(DEPTH):
        j = l // 2
        is_hgrn = l % 2 == 0
        need_ctx_out = l < DEPTH - 1
        mod = silu_c @ ada_w[l] + ada_b[l]
        sh1, sc1, g1, sh2, sc2, g2 = [m[:, None, :] for m in jnp.split(mod, N_MOD, axis=-1)]
        h = _modulate(_rmsnorm(x, norm_w[l, 0]), sh1, sc1)
        if is_hgrn or need_ctx_out:
            cmod = silu_cc @ ada_w[l] + ada_b[l]
            csh1, csc1, cg1, csh2, csc2, cg2 = jnp.split(cmod, N_MOD, axis=-1)
            hc = _modulate(_rmsnorm(ctx, norm_w[l, 0]), csh1, csc1)
        if is_hgrn:
            y, yc = _hgrn2_mixer(h, hc, hgrn_w_in[j], hgrn_w_out[j], hgrn_gnorm[j],
                                 lower_bounds[j], need_ctx_out)
        else:
            y = _short_conv_mixer(h, conv_w_in[j], conv_w[j], conv_w_out[j], rows)
            yc = _short_conv_mixer(hc, conv_w_in[j], conv_w[j], conv_w_out[j], None) if need_ctx_out else None
        x = x + g1 * _rmsnorm(y, norm_w[l, 1])
        hf = _modulate(_rmsnorm(x, norm_w[l, 2]), sh2, sc2)
        x = x + g2 * _rmsnorm(_swiglu(hf, ffn_w_in[l], ffn_w_out[l]), norm_w[l, 3])
        if need_ctx_out:
            ctx = ctx + cg1 * _rmsnorm(yc, norm_w[l, 1])
            hfc = _modulate(_rmsnorm(ctx, norm_w[l, 2]), csh2, csc2)
            ctx = ctx + cg2 * _rmsnorm(_swiglu(hfc, ffn_w_in[l], ffn_w_out[l]), norm_w[l, 3])
    return x


_drawn_inputs = setup_inputs


def setup_inputs(seed=0):
    import zlib

    import numpy as np

    out = dict(_drawn_inputs(seed))
    spreads = {}
    factors = {'ctx': 37.297, 'c_ctx': 26.881, 'hgrn_gnorm': 8.731}
    for name, (base, spread) in spreads.items():
        noise = np.random.default_rng([zlib.crc32(name.encode()), seed]).standard_normal(out[name].shape)
        drawn = base * np.exp(spread * noise) if base else spread * noise
        out[name] = __import__('jax').numpy.asarray(drawn.astype(out[name].dtype))
    for name, factor in factors.items():
        out[name] = (out[name] * factor).astype(out[name].dtype)
    return out
```

```python
from contextlib import ExitStack

import concourse.bass as bass
from concourse import mybir

F32 = mybir.dt.float32
F32R = mybir.dt.float32r
U8 = mybir.dt.uint8
ACT = mybir.ActivationFunctionType
ALU = mybir.AluOpType

P = 128
D = 1024
KB = D // P
SEQ, CTX = 1024, 256
HALF = 512
GRID_W = 64
HEADS = D // P
FFN = 2816
FFN_GROUPS = FFN // (2 * P)
LAT = SEQ // P
CCH = CTX // P
CHUNKS = CCH + LAT
ALL = CHUNKS * P
LEVELS = 7
EPS = 1e-6
F_FLOOR = 1e-6
FWD, BWD = 0, 1
HEAD_PARTS = (2, 3, 0, 1, 4)
HEAD_PANELS = len(HEAD_PARTS)
ADA_START = 16
ADA_GROUP = 4
G_OUT = HEADS
G_CONV = G_OUT + 4
FFN_HIDDEN_PANELS, FFN_OUT_PANELS = 4, 2

HEAD_ADA = ((), (0, 1), (), (2, 3), ())
CONV_ADA = ((0, 1), (2,), (3,))

N_HEADS = 0
N_HGRN_OUT = N_HEADS + HEADS * HEAD_PANELS
N_FFN0 = N_HGRN_OUT + KB
N_CONV = N_FFN0 + FFN_GROUPS * 6
N_CONV_OUT = N_CONV + KB * 3
N_FFN1 = N_CONV_OUT + KB
N_PANELS = N_FFN1 + FFN_GROUPS * 6
O_HEADS = 0
O_HGRN_OUT = O_HEADS + 2 * HEADS * HEAD_PANELS
O_FFN0 = O_HGRN_OUT + 2 * KB
O_CONV = O_FFN0 + 8 * FFN_GROUPS
O_CONV_OUT = O_CONV + 6 * KB
O_FFN1 = O_CONV_OUT + 2 * KB

SCAN_BANKS = (4, 5)
U_V, U_DIAG, U_LEVEL, U_KF, U_KVF, U_KB, U_KVB, U_O, U_BC = 0, 3, 5, 19, 22, 25, 28, 31, 33
SCAN_USES = 35
ACT_EVACS = 9
NSQ = 2 * KB
BY_BLOCK = (0, 1, 5)
AFTER_FFN = (3, 7)
SCORE_EVACS = 16
STATE_OPS = 9
STATE_AT = (4, 8, 9)


def scan_readers(use):
    if use < U_DIAG:
        return [("scan_evac", ACT_EVACS, use)]
    if use < U_KF:
        return [("scores_evac", SCORE_EVACS, use - U_DIAG)]
    if use < U_KVF:
        return [("scan_evac", ACT_EVACS, 3 + use - U_KF)]
    if use < U_KB:
        return [("state_f", STATE_OPS, STATE_AT[use - U_KVF] - 1)]
    if use < U_KVB:
        return [("scan_evac", ACT_EVACS, 6 + use - U_KB)]
    if use < U_O:
        return [("state_b", STATE_OPS, STATE_AT[use - U_KVB] - 1)]
    if use < U_BC:
        return [("o_gated", 2, use - U_O)]
    return [("mix_ready", 2, use - U_BC)]


def updated(sub, m, half):
    return 2 * KB * (2 * sub + half) + min(2 * m + 3, 2 * KB)


def place(norm, j):
    return (j // 2, j % 2) if norm in BY_BLOCK else (j % KB, j // KB)


def pick(t, i):
    return t[i] if isinstance(i, int) else t[bass.ds(i, 1)].rearrange("o p n -> (o p) n")


def state_chunks(d):
    if d == FWD:
        return list(range(CHUNKS - 1))
    return list(range(CCH - 1, -1, -1)) + list(range(CHUNKS - 1, CCH, -1))


def build_trunk(nc, x, ctx, cond, ada_start, ada, ada_bias, norm_w, lb_raw, gnorm, conv_w,
                w_hgrn_in, w_hgrn_out, w_conv_in, w_conv_out, w_ffn_in, w_ffn_out, out):
    base = (nc.sbuf_base + 31) // 32 * 32

    def at(name, kib, shape, dt=F32):
        return nc.alloc_sbuf_tensor_at(name, shape, dt, offset=base + int(kib * 1024))

    h_hi = at("h_hi", 0, [P, KB, SEQ], F32R)
    h_lo = at("h_lo", 32, [P, KB, SEQ], F32R)
    ada_first = at("ada_first", 0, [P, ADA_START, D])
    mix = at("mix", 64, [P, KB, SEQ])
    y = at("y", 64, [P, KB, SEQ])
    w_raw = at("w_raw", 96, [P, 2, D])
    w_hi = at("w_hi", 104, [P, 2, D], F32R)
    w_lo = at("w_lo", 112, [P, 2, D], F32R)
    ada_raw = at("ada_raw", 120, [P, 2, D])
    xt = at("xt", 128, [P, KB, SEQ])
    hc_hi = at("hc_hi", 160, [P, KB, CTX], F32R)
    hc_lo = at("hc_lo", 168, [P, KB, CTX], F32R)
    ctxt = at("ctxt", 176, [P, KB, CTX])
    scaled = at("scaled", 184, [P, 4, HALF])
    modulated = at("modulated", 192, [P, 4, HALF])
    squares = at("squares", 204, [P, 4, HALF])
    hidden_hi = [at(f"hidden_hi{i}", 160 + 16 * i, [P, 2, SEQ], F32R) for i in range(2)]
    hidden_lo = [at(f"hidden_lo{i}", 168 + 16 * i, [P, 2, SEQ], F32R) for i in range(2)]
    gate_act = at("gate_act", 192, [P, 2, HALF])
    up_copy = at("up_copy", 196, [P, 2, HALF])
    hidden = at("hidden", 200, [P, 2, HALF])
    conv_u = at("conv_u", 160, [P, SEQ])
    conv_v = at("conv_v", 164, [P, SEQ])
    conv_c = at("conv_c", 168, [P, SEQ])
    conv_x = at("conv_x", 172, [P, SEQ])
    conv_b = at("conv_b", 176, [P, SEQ])
    z = [at("z_f", 128, [P, ALL]), at("z_b", 133, [P, ALL])]
    q = at("q", 138, [P, SEQ])
    g = at("g", 142, [P, SEQ])
    v_t = at("v_t", 146, [P, ALL])
    v_tok = at("v_tok", 151, [P, CHUNKS, P])
    scores = at("scores", 156, [P, LAT, P])
    gates = [at("gates_f", 176, [P, ALL]), at("gates_b", 181, [P, ALL])]
    k = [at("k_f", 186, [P, ALL]), at("k_b", 191, [P, ALL])]
    qd = [at("q_f", 196, [P, SEQ]), at("q_b", 200, [P, SEQ])]
    totals = [at("totals_f", 204, [P, ALL // 2]), at("totals_b", 206.5, [P, ALL // 2])]
    k_sum = at("k_sum", 209, [P, SEQ])
    k_tok = at("k_tok", 209, [P, CHUNKS - 1, P])
    o_sq = at("o_sq", 209, [P, SEQ])
    totals_even = [at("totals_even_f", 176, [P, ALL // 4]), at("totals_even_b", 181, [P, ALL // 4])]
    state = [at("state_f_t", 176, [P, LAT, P]), at("state_b_t", 181, [P, LAT, P])]
    ident = at("ident", 214, [P, P])
    masks = at("masks", 214.5, [P, 2 * LEVELS, P // 2], U8)
    mask_f32 = at("mask_f32", 204, [P, 2 * LEVELS, P // 2])
    small_at = [215.5]

    def small(name, n):
        t = at(name, small_at[0], [P, n])
        small_at[0] += (4 * n + 31) // 32 * 32 / 1024
        return t

    ones = small("ones", 1)
    zero = small("zero", 1)
    cond_in = small("cond_in", 2 * KB)
    silu_cond = small("silu_cond", 2 * KB)
    bias = small("bias", 12 * KB)
    mods = small("mods", 12 * KB)
    cmods = small("cmods", 2 * KB)
    nw = small("nw", 8 * KB)
    lbr = small("lbr", KB)
    lb_exp = small("lb_exp", 3 * KB)
    lb = small("lb", KB)
    one_minus_lb = small("one_minus_lb", KB)
    gn = small("gn", 1)
    cw = small("cw", 3 * KB)
    in_scale = small("in_scale", 5 * KB)
    out_scale = small("out_scale", 4 * KB)
    var = small("var", KB)
    inv_var = small("inv_var", KB)
    rstd = small("rstd", KB)
    cvar = small("cvar", 2 * CCH)
    crstd = small("crstd", CCH)
    ada_acc = small("ada_acc", HALF)
    ovar = small("ovar", 2 * LAT)
    orstd = small("orstd", LAT)
    assert base + (small_at[0]) * 1024 <= nc.sbuf_usable_end

    ctx_mgr = ExitStack()
    with ctx_mgr:
        psum = ctx_mgr.enter_context(nc.psum_tensor("psum", [P, 8 * HALF], F32))
        names = """panel_loaded0 panel_loaded1 w_hi_done panel_split panel_started
            gemm_full gemm_evac ctx_full ctx_evac
            ada_first0 ada_first1 ada_first2 ada_first3 ada_loaded0 ada_loaded1 ada_step ada_first_done ada_summed ada_evac
            small_loaded x_loaded ctx_loaded x_reloaded stored
            masks_f32 consts silu_done cmod_done params
            squares_ready squares_used var_done rstd_ready bc_full scaled_done x_updated
            modulated_done h_hi_done h_ready
            csq_ready csq_used cvar_done crstd_ready cbc_full cscaled cmodulated chi_done hc_ready
            sigmoids gates_done diag_ready scan_f scan_b scan_full scan_evac scores_evac state_f state_b
            gate_sig gs_ready o_squared o_gated o_sum_full ovar_done orstd_ready mix_ready mods_ready
            mix_hi mix_split
            hidden_done hidden_hi_done hidden_ready partial_full partial_evac y_zeroed
            conv_done""".split()
        S = {n: ctx_mgr.enter_context(nc.semaphore(n)) for n in names}
        scan_sem = [S["scan_f"], S["scan_b"]]
        state_sem = [S["state_f"], S["state_b"]]
        credit = {n: c for n, c in (("scan_evac", ACT_EVACS), ("scores_evac", SCORE_EVACS),
                                    ("state_f", STATE_OPS), ("state_b", STATE_OPS), ("o_squared", 2),
                                    ("o_gated", 2), ("mix_ready", 2))}

        def bank(i, a=0, b=HALF):
            return psum[:, i * HALF + a:i * HALF + b]

        csum_out = bank(2, 0, CCH)
        ada_first_out = bank(3, 0, 2 * ADA_START)
        ctx_out = bank(6, 0, CTX)
        sum_out = [bank(0 if norm in AFTER_FFN else 6, 0, KB) for norm in range(8)]
        ada_out = bank(7, 0, ADA_GROUP)
        o_sum_out = bank(7, 64, 64 + LAT)

        def bc(norm, half):
            return (2 if norm in AFTER_FFN else 4) + half

        def chunk(t, c):
            return t[:, c * P:(c + 1) * P]

        def cols_of(half):
            return slice(half * HALF, (half + 1) * HALF)

        def lat(t):
            return t[:, CTX:ALL]

        def halves(ap, b):
            return ap.rearrange("p (n two b) -> p n two b", two=2, b=b)

        Q_HALF, K_HALF = (1, 0), (0, 1)

        def total_of(d, i):
            n = ALL >> i
            if i == 0:
                return gates[d][:, :]
            return (totals[d] if i % 2 else totals_even[d])[:, 0:n]

        block = ctx_mgr.enter_context(nc.Block())

        @block.sync
        def _(sp):
            def small_load(dst, src):
                sp.dma_start(dst, src).then_inc(S["small_loaded"], 16)

            def panel(n, slot, src):
                if not (isinstance(n, int) and n < 2):
                    sp.wait_ge(S["panel_split"], n - 1)
                sp.dma_start(w_raw[:, slot, :], src).then_inc(S[f"panel_loaded{slot}"], 16)

            def ada_panel(m, slot):
                if not (isinstance(m, int) and m < 2):
                    sp.wait_ge(S["ada_step"], m * 2 - 2)
                sp.dma_start(ada_raw[:, slot, :], pick(ada, m)).then_inc(S[f"ada_loaded{slot}"], 16)

            small_load(cond_in[:, :], cond)
            small_load(bias[:, :], ada_bias)
            small_load(nw[:, :], norm_w)
            small_load(lbr[:, :], lb_raw)
            small_load(gn[:, :], gnorm)
            small_load(cw[:, :], conv_w)
            for j in range(4):
                m = KB // 4
                sp.dma_start(xt[:, j * m:(j + 1) * m, :],
                             x[j * m:(j + 1) * m].rearrange("k p t -> p k t")).then_inc(S["x_loaded"], 16)
                sp.wait_ge(S["x_loaded"], 16 * (j + 1))
            sp.dma_start(ctxt[:, :, :], ctx.rearrange("k p t -> p k t")).then_inc(S["ctx_loaded"], 16)

            def head_loads(h, parity):
                n = N_HEADS + h * HEAD_PANELS
                for i in range(HEAD_PANELS):
                    panel(n + i, (parity + i) % 2, pick(w_hgrn_in, n + i))
                    for a in HEAD_ADA[i]:
                        ada_panel(h * ADA_GROUP + a, a % 2)

            head_loads(0, 0)
            with sp.Fori(0, HEADS // 2 - 1) as i:
                head_loads(i * 2 + 1, 1)
                head_loads(i * 2 + 2, 0)
            head_loads(HEADS - 1, 1)

            def stream(n0, count, src):
                with sp.Fori(0, count // 2) as i:
                    panel(i * 2 + n0, 0, pick(src, i * 2))
                    panel(i * 2 + (n0 + 1), 1, pick(src, i * 2 + 1))

            def hgrn_out_panel(i, slot):
                panel(i + N_HGRN_OUT, slot, pick(w_hgrn_out, i))
                for t in range(2):
                    ada_panel(i * 2 + (ADA_GROUP * G_OUT + t), t)

            hgrn_out_panel(0, 0)
            panel(N_HGRN_OUT + 1, 1, w_hgrn_out[1])
            sp.wait_ge(S["mix_ready"], credit["mix_ready"] + 2 * HEADS)
            sp.dma_start(xt[:, :, :], x.rearrange("k p t -> p k t")).then_inc(S["x_reloaded"], 16)
            for t in range(2):
                ada_panel(ADA_GROUP * G_OUT + 2 + t, t)
            with sp.Fori(1, KB // 2) as i:
                hgrn_out_panel(i * 2, 0)
                hgrn_out_panel(i * 2 + 1, 1)

            def ffn_loads(n0, w_in, w_out):
                def hidden_panels(n, grp):
                    for j in range(FFN_HIDDEN_PANELS):
                        panel(n + j, j % 2, pick(w_in, grp * 4 + j))

                def out_panels(n, grp):
                    for j in range(FFN_OUT_PANELS):
                        panel(n + j, j % 2, pick(w_out, grp * 2 + j))

                for j in range(FFN_HIDDEN_PANELS):
                    panel(n0 + j, j % 2, w_in[j])
                with sp.Fori(1, FFN_GROUPS) as i:
                    hidden_panels(i * 6 + (n0 - 2), i)
                    out_panels(i * 6 + (n0 + 2), i - 1)
                for j in range(FFN_OUT_PANELS):
                    r = 2 * FFN_GROUPS - 2 + j
                    panel(n0 + 6 * FFN_GROUPS - 2 + j, j % 2, w_out[r])

            ffn_loads(N_FFN0, w_ffn_in[0], w_ffn_out[0])

            with sp.Fori(0, KB // 2) as i:
                for e in range(2):
                    blk = i * 2 + e
                    for j in range(3):
                        panel(blk * 3 + (N_CONV + j), (e + j) % 2, pick(w_conv_in, blk * 3 + j))
                        for a in CONV_ADA[j]:
                            ada_panel(blk * ADA_GROUP + (ADA_GROUP * G_CONV + a), a % 2)
            stream(N_CONV_OUT, KB, w_conv_out)
            ffn_loads(N_FFN1, w_ffn_in[1], w_ffn_out[1])

            for half in range(2):
                for m in range(KB):
                    sp.wait_ge(S["x_updated"], updated(3, m, half))
                    sp.dma_start(out[m][:, cols_of(half)], xt[:, m, cols_of(half)]).then_inc(S["stored"], 16)
            sp.wait_ge(S["stored"], 16 * 2 * KB)

        @block.gpsimd
        def _(pool):
            pool.memset(ones[:, :], 1.0).then_inc(S["consts"], 1)
            pool.memset(zero[:, :], 0.0).then_inc(S["consts"], 1)
            pool.memset(ident[:, :], 0.0).then_inc(S["consts"], 1)
            pool.memset(mask_f32[:, :, :], 1.0).then_inc(S["consts"], 1)
            pool.wait_ge(S["consts"], 4)
            pool.affine_select(out=ident[:, :], in_=ident[:, :], compare_op=ALU.not_equal, fill=1.0,
                               base=0, pattern=[[-1, P]], channel_multiplier=1).then_inc(S["consts"], 1)
            for n, (i, d) in enumerate((i, d) for i in range(LEVELS) for d in (FWD, BWD)):
                b = 1 << i
                m = mask_f32[:, d * LEVELS + i, :].rearrange("p (n b) -> p n b", b=b)
                pool.affine_select(out=m, in_=m, compare_op=ALU.is_ge, fill=0.0, base=-b * K_HALF[d],
                                   pattern=[[-2 * b, P // (2 * b)], [0, b]], channel_multiplier=1
                                   ).then_inc(S["masks_f32"], 1)
                pool.wait_ge(S["masks_f32"], 2 * n + 1)
                pool.affine_select(out=m, in_=m, compare_op=ALU.is_ge, fill=0.0,
                                   base=b * K_HALF[d] + b - 1,
                                   pattern=[[2 * b, P // (2 * b)], [0, b]], channel_multiplier=-1
                                   ).then_inc(S["masks_f32"], 1)
            with pool.Fori(0, N_PANELS // 2) as i:
                for slot in range(2):
                    pool.wait_ge(S[f"panel_loaded{slot}"], i * 16 + 16)
                    pool.wait_ge(S["panel_started"], i * 2 + slot + 1)
                    pool.tensor_tensor(w_hi[:, slot, :], w_raw[:, slot, :],
                                       zero[:, 0:1].broadcast_to([P, D]), ALU.add).then_inc(S["w_hi_done"], 1)
                    pool.wait_ge(S["w_hi_done"], i * 2 + slot + 1)
                    pool.tensor_tensor(w_lo[:, slot, :], w_raw[:, slot, :], w_hi[:, slot, :],
                                       ALU.subtract).then_inc(S["panel_split"], 1)

        @block.tensor
        def _(pe):
            def products(out_ap, slot, kb, rhs_hi, rhs_lo, first, last):
                a, b = kb * P, (kb + 1) * P
                pe.matmul(out_ap, w_hi[:, slot, a:b], rhs_hi, start=first, stop=False)
                pe.matmul(out_ap, w_hi[:, slot, a:b], rhs_lo, start=False, stop=False)
                return pe.matmul(out_ap, w_lo[:, slot, a:b], rhs_hi, start=False, stop=last)

            def panel_begin(n):
                pe.wait_ge(S["panel_split"], n + 1)

            def gemm_blocks(n, o, slot, pair, operand_wait=None):
                for half in range(2):
                    dst = bank(2 * pair + half)
                    cols = slice(half * HALF, (half + 1) * HALF)
                    if half == 0:
                        panel_begin(n)
                    pe.wait_ge(S["gemm_evac"], o + half + 1)
                    for kb in range(KB):
                        if operand_wait is not None:
                            operand_wait(half, kb)
                        if half == 0 and kb == 0:
                            pe.matmul(dst, w_hi[:, slot, 0:P], h_hi[:, 0, cols], start=True,
                                      stop=False).then_inc(S["panel_started"], 1)
                            pe.matmul(dst, w_hi[:, slot, 0:P], h_lo[:, 0, cols], start=False, stop=False)
                            mm = pe.matmul(dst, w_lo[:, slot, 0:P], h_hi[:, 0, cols], start=False, stop=False)
                        else:
                            mm = products(dst, slot, kb, h_hi[:, kb, cols], h_lo[:, kb, cols],
                                          kb == 0, kb == KB - 1)
                        if kb == KB - 1:
                            mm.then_inc(S["gemm_full"], 1)
                        yield

            def gemm_panel(n, o, slot, pair, operand_wait=None):
                for _ in gemm_blocks(n, o, slot, pair, operand_wait):
                    pass

            def pair_by_halves(n, o, operand_wait):
                for half in range(2):
                    for slot in range(2):
                        dst = bank(2 * half + slot)
                        if half == 0:
                            panel_begin(n + slot)
                        pe.wait_ge(S["gemm_evac"], o + 2 * half + slot + 1)
                        for kb in range(KB):
                            operand_wait(half, slot, kb)
                            rhs_hi, rhs_lo = h_hi[:, kb, cols_of(half)], h_lo[:, kb, cols_of(half)]
                            if kb == 0 and slot == half:
                                pe.matmul(dst, w_hi[:, slot, 0:P], rhs_hi, start=True,
                                          stop=False).then_inc(S["panel_started"], 1)
                                pe.matmul(dst, w_hi[:, slot, 0:P], rhs_lo, start=False, stop=False)
                                mm = pe.matmul(dst, w_lo[:, slot, 0:P], rhs_hi, start=False, stop=False)
                            else:
                                mm = products(dst, slot, kb, rhs_hi, rhs_lo, kb == 0, kb == KB - 1)
                        mm.then_inc(S["gemm_full"], 1)

            def square_sums(norm, j):
                m, half = place(norm, j)
                if j == (NSQ - 1 if norm in BY_BLOCK[1:] else KB) and norm > 0:
                    pe.wait_ge(S["var_done"], 4 * norm + 1)
                pe.wait_ge(S["squares_ready"], NSQ * norm + j + 1)
                first = j == 0 or (j == KB and norm not in BY_BLOCK)
                for c in range(4):
                    mm = pe.matmul(sum_out[norm][:, 4 * half + c:4 * half + c + 1],
                                   chunk(squares[:, j % 4, :], c), ones[:, :],
                                   start=(first and c == 0), stop=(m == KB - 1), skip_group_check=True)
                mm.then_inc(S["squares_used"], 1)

            def broadcast_rstd(norm, half):
                pe.wait_ge(S["rstd_ready"], 2 * norm + half + 1)
                b = bc(norm, half)
                for c in range(4 * half, 4 * half + 4):
                    mm = pe.matmul(bank(b, (c % 4) * P, (c % 4 + 1) * P), rstd[:, c:c + 1].broadcast_to([P, P]), ident[:, :],
                                   start=True, stop=True)
                mm.then_inc(S["bc_full"], 1)

            def ada_sums(g):
                pe.wait_ge(S["ada_step"], g * 8 + 8)
                if not (isinstance(g, int) and g == 0):
                    pe.wait_ge(S["ada_evac"], g)
                for j in range(ADA_GROUP):
                    mm = pe.matmul(ada_out[:, j:j + 1], ada_acc[:, j * P:(j + 1) * P], ones[:, :],
                                   start=True, stop=True)
                mm.then_inc(S["ada_summed"], 1)

            pe.sem_inc(S["scan_full"], SCAN_USES)
            pe.sem_inc(S["panel_started"], 1)
            pe.sem_inc(S["ada_summed"], 1)
            pe.wait_ge(S["consts"], 5)
            for j in range(NSQ):
                square_sums(0, j)
            for part in range(2):
                pe.wait_ge(S["csq_ready"], part + 1)
                for j in range(4):
                    for c in range(CCH):
                        mm = pe.matmul(csum_out[:, c:c + 1],
                                       chunk(squares[:, 2 * part + j // 2, :], (j % 2) * CCH + c), ones[:, :],
                                       start=(part == 0 and j == 0 and c == 0), stop=(part == 1 and j == 3),
                                       skip_group_check=True)
                mm.then_inc(S["csq_used"], 1)
            for half in range(2):
                broadcast_rstd(0, half)
            pe.wait_ge(S["crstd_ready"], 1)
            for c in range(CCH):
                mm = pe.matmul(bank(7, c * P, (c + 1) * P), crstd[:, c:c + 1].broadcast_to([P, P]),
                               ident[:, :], start=True, stop=True)
            mm.then_inc(S["cbc_full"], 1)
            pe.wait_ge(S["silu_done"], 1)
            for m in range(ADA_START):
                if m % 4 == 0:
                    pe.wait_ge(S[f"ada_first{m // 4}"], 16)
                for kb in range(KB):
                    mm = pe.matmul(ada_first_out[:, 2 * m:2 * m + 2], ada_first[:, m, kb * P:(kb + 1) * P],
                                   silu_cond[:, 2 * kb:2 * kb + 2], start=(kb == 0), stop=(kb == KB - 1))
            mm.then_inc(S["ada_first_done"], 1)

            pe.wait_ge(S["cscaled"], 1)

            def scan_use(hh, use):
                earlier = [u for u in range(use) if u % 2 == use % 2]
                if earlier:
                    for name, per_head, idx in scan_readers(earlier[-1]):
                        pe.wait_ge(S[name], hh * per_head + (credit[name] + idx + 1))
                else:
                    before = [u for u in range(SCAN_USES) if u % 2 == use % 2][-1]
                    for name, per_head, idx in scan_readers(before):
                        pe.wait_ge(S[name], hh * per_head + (credit[name] - per_head + idx + 1))
                return SCAN_BANKS[use % 2]

            def transposes(hh, use, src, chunks):
                b = scan_use(hh, use)
                for j, c in enumerate(chunks):
                    mm = pe.transpose(bank(b, j * P, (j + 1) * P), src[:, c * P:(c + 1) * P], ident[:, :])
                mm.then_inc(S["scan_full"], 1)

            def v_transposes(hh, part):
                if part == 0:
                    pe.wait_ge(S["gemm_evac"], hh * 10 + (4 + O_HEADS + 8))
                    pe.wait_ge(S["ctx_evac"], hh * 3 + (1 + 3))
                transposes(hh, U_V + part, v_t, range(4 * part, min(4 * part + 4, CHUNKS)))

            def diagonal(hh, part):
                pe.wait_ge(S["diag_ready"], hh + 1)
                b = scan_use(hh, U_DIAG + part)
                for c in range(4 * part, 4 * part + 4):
                    mm = pe.matmul(bank(b, (c % 4) * P, (c % 4 + 1) * P), chunk(k_sum, c), chunk(q, c),
                                   start=True, stop=True)
                mm.then_inc(S["scan_full"], 1)

            def level(hh, i, d):
                b = scan_use(hh, U_LEVEL + 2 * i + d)
                pe.wait_ge(scan_sem[d], hh * 22 + (1 if i == 0 else 3 * i))
                for c in range(LAT):
                    qs = halves(chunk(qd[d], c), 1 << i)[:, :, Q_HALF[d], :]
                    mm = pe.matmul(bank(b, c * 64, (c + 1) * 64), chunk(lat(k[d]), c), qs,
                                   start=True, stop=True)
                mm.then_inc(S["scan_full"], 1)

            def key_transposes(hh, d, part):
                if part == 0:
                    pe.wait_ge(scan_sem[d], hh * 22 + 22)
                transposes(hh, (U_KF, U_KB)[d] + part, k[d], state_chunks(d)[4 * part:4 * part + 4])

            def key_values(hh, d, part):
                pe.wait_ge(S["scan_evac"], hh * ACT_EVACS + (ACT_EVACS + 3 + 3 * d + part + 1))
                b = scan_use(hh, (U_KVF, U_KVB)[d] + part)
                for j, c in enumerate(state_chunks(d)[4 * part:4 * part + 4]):
                    mm = pe.matmul(bank(b, j * P, (j + 1) * P), k_tok[:, 4 * part + j, :], v_tok[:, c, :],
                                   start=True, stop=True)
                mm.then_inc(S["scan_full"], 1)

            def outputs(hh, part):
                pe.wait_ge(S["scores_evac"], hh * SCORE_EVACS + 2 * SCORE_EVACS)
                for d in (FWD, BWD):
                    pe.wait_ge(state_sem[d], hh * STATE_OPS + 2 * STATE_OPS)
                b = scan_use(hh, U_O + part)
                for c in range(4 * part, 4 * part + 4):
                    dst = bank(b, (c % 4) * P, (c % 4 + 1) * P)
                    pe.matmul(dst, v_tok[:, CCH + c, :], scores[:, c, :], start=True, stop=False)
                    pe.matmul(dst, state[FWD][:, c, :], chunk(qd[FWD], c), start=False, stop=False)
                    mm = pe.matmul(dst, state[BWD][:, c, :], chunk(qd[BWD], c), start=False, stop=True)
                mm.then_inc(S["scan_full"], 1)

            def output_sums(hh):
                pe.wait_ge(S["o_squared"], hh * 2 + (credit["o_squared"] + 2))
                for c in range(LAT):
                    mm = pe.matmul(o_sum_out[:, c:c + 1], chunk(o_sq, c), ones[:, :], start=True, stop=True)
                mm.then_inc(S["o_sum_full"], 1)

            def output_rstd(hh, part):
                pe.wait_ge(S["orstd_ready"], hh + 1)
                b = scan_use(hh, U_BC + part)
                for c in range(4 * part, 4 * part + 4):
                    mm = pe.matmul(bank(b, (c % 4) * P, (c % 4 + 1) * P),
                                   orstd[:, c:c + 1].broadcast_to([P, P]), ident[:, :], start=True, stop=True)
                mm.then_inc(S["scan_full"], 1)

            def head(gemm_of, parity, scan_of, first=False):
                hg, hs = gemm_of, scan_of

                def context_block(i, ci):
                    pe.wait_ge(S["ctx_evac"], hg * 3 + (ci + 1))
                    for kb in range(KB):
                        mm = products(ctx_out, (parity + i) % 2, kb, hc_hi[:, kb, :], hc_lo[:, kb, :],
                                      kb == 0, kb == KB - 1)
                    mm.then_inc(S["ctx_full"], 1)

                def steps():
                    if hg is None:
                        while True:
                            yield
                    for i in range(HEAD_PANELS):
                        wait = (lambda half, kb: pe.wait_ge(S["h_ready"], KB * half + kb + 1)) if first and i == 0 else None
                        n, o = hg * HEAD_PANELS + (N_HEADS + i), hg * 10 + (O_HEADS + 2 * i)
                        yield from gemm_blocks(n, o, (parity + i) % 2, (parity + i) % 2, wait)
                        if i in (0, 1, 3):
                            if first and i == 0:
                                pe.wait_ge(S["hc_ready"], 1)
                            context_block(i, {0: 0, 1: 1, 3: 2}[i])
                    if hs is not None:
                        pe.wait_ge(S["ovar_done"], hs * 2 + 1)
                    ada_sums(hg)

                it = steps()

                def slots(n):
                    for _ in range(n):
                        next(it)

                if hs is not None:
                    slots(1)
                    for part in range(3):
                        v_transposes(hs, part)
                        slots(1)
                    slots(10)
                    diagonal(hs, 0)
                    slots(1)
                    diagonal(hs, 1)
                    slots(1)
                    for i in range(LEVELS):
                        for d in (FWD, BWD):
                            level(hs, i, d)
                            slots(2)
                    slots(3)
                    for d in (FWD, BWD):
                        for part in range(3):
                            key_transposes(hs, d, part)
                            slots(1)
                        for part in range(3):
                            key_values(hs, d, part)
                            slots(1)
                    slots(4)
                    for part in range(2):
                        outputs(hs, part)
                        slots(1)
                    slots(1)
                    output_sums(hs)
                    slots(5)
                    for part in range(2):
                        output_rstd(hs, part)
                        slots(1)
                if hg is not None:
                    for _ in it:
                        pass

            head(0, 0, None, first=True)
            with pe.Fori(0, HEADS // 2 - 1) as i:
                head(i * 2 + 1, 1, i * 2)
                head(i * 2 + 2, 0, i * 2 + 1)
            head(HEADS - 1, 1, HEADS - 2)
            head(None, 0, HEADS - 1)

            def out_projection(n0, o0, norm, split_before, group=None):
                pair_by_halves(n0, o0, lambda half, slot, kb: pe.wait_ge(
                    S["mix_split"], split_before + KB * half + kb + 1))
                square_sums(norm, 0)
                square_sums(norm, 1)
                if group is not None:
                    ada_sums(group)
                with pe.Fori(1, KB // 2 - 1) as i:
                    gemm_panel(i * 2 + n0, i * 4 + o0, 0, 0)
                    sums_in_loop(norm, i * 4 - 2, 2)
                    gemm_panel(i * 2 + (n0 + 1), i * 4 + (o0 + 2), 1, 1)
                    sums_in_loop(norm, i * 4, 0)
                    if group is not None:
                        ada_sums(i + group)
                n, o = n0 + KB - 2, o0 + 2 * KB - 4
                gemm_panel(n, o, 0, 0)
                square_sums(norm, NSQ - 6)
                square_sums(norm, NSQ - 5)
                if group is not None:
                    ada_sums(group + 3)
                for step, _ in enumerate(gemm_blocks(n + 1, o + 2, 1, 1)):
                    if step in (3, 4):
                        square_sums(norm, NSQ - 7 + step)
                    if step == KB + 3:
                        square_sums(norm, NSQ - 2)
                    if step == KB + 6:
                        broadcast_rstd(norm, 0)
                square_sums(norm, NSQ - 1)
                broadcast_rstd(norm, 1)

            def sums_in_loop(norm, j, slot):
                for half in range(2):
                    pe.wait_ge(S["squares_ready"], j + (NSQ * norm + half + 1))
                    for c in range(4):
                        mm = pe.matmul(sum_out[norm][:, 4 * half + c:4 * half + c + 1],
                                       chunk(squares[:, slot + half, :], c), ones[:, :],
                                       start=False, stop=False, skip_group_check=True)
                    mm.then_inc(S["squares_used"], 1)

            def next_norm(norm):
                for j in range(KB):
                    square_sums(norm, j)
                broadcast_rstd(norm, 0)

            def start_wait(norm, before):
                def wait(half, slot, kb):
                    if half == 0 and slot == 0:
                        square_sums(norm, KB + kb)
                    if slot == 0:
                        pe.wait_ge(S["h_ready"], before + KB * half + kb + 1)
                    if half == 0 and slot == 1 and kb == 3:
                        broadcast_rstd(norm, 1)
                return wait

            def ffn(f, n0, o0, wait, norm):
                def hidden_panels(n, o, first=0):
                    for j in range(first, FFN_HIDDEN_PANELS):
                        gemm_panel(n + j, o + 2 * j, j % 2, j % 2)

                def out_panels(n, grp, buf):
                    pe.wait_ge(S["hidden_ready"], grp * 4 + (4 * FFN_GROUPS * f + 4))
                    for j in range(FFN_OUT_PANELS):
                        panel_begin(n + j)
                        for m in range(4):
                            for half in range(2):
                                idx = j * 8 + m * 2 + half
                                cols = slice(half * HALF, (half + 1) * HALF)
                                dst = bank(4 + idx % 4)
                                pe.wait_ge(S["partial_evac"], grp * 16 + (16 * FFN_GROUPS * f + idx + 1))
                                for kb in range(2):
                                    a = (kb * 4 + m) * P
                                    mm = pe.matmul(dst, w_hi[:, j, a:a + P], hidden_hi[buf][:, kb, cols],
                                                   start=(kb == 0), stop=False)
                                    if m == 0 and half == 0 and kb == 0:
                                        mm.then_inc(S["panel_started"], 1)
                                    pe.matmul(dst, w_hi[:, j, a:a + P], hidden_lo[buf][:, kb, cols],
                                              start=False, stop=False)
                                    mm = pe.matmul(dst, w_lo[:, j, a:a + P], hidden_hi[buf][:, kb, cols],
                                                   start=False, stop=(kb == 1))
                                mm.then_inc(S["partial_full"], 1)

                def last_out_panels(n, grp, buf):
                    base_f = 16 * FFN_GROUPS * f + 16 * grp
                    pe.wait_ge(S["hidden_ready"], grp * 4 + (4 * FFN_GROUPS * f + 4))
                    for half in range(2):
                        cols = cols_of(half)
                        for j in range(FFN_OUT_PANELS):
                            if half == 0:
                                panel_begin(n + j)
                            for m in range(4):
                                idx = half * 8 + j * 4 + m
                                dst = bank(4 + idx % 4)
                                pe.wait_ge(S["partial_evac"], base_f + idx + 1)
                                for kb in range(2):
                                    a = (kb * 4 + m) * P
                                    mm = pe.matmul(dst, w_hi[:, j, a:a + P], hidden_hi[buf][:, kb, cols],
                                                   start=(kb == 0), stop=False)
                                    if m == 0 and half == j and kb == 0:
                                        mm.then_inc(S["panel_started"], 1)
                                    pe.matmul(dst, w_hi[:, j, a:a + P], hidden_lo[buf][:, kb, cols],
                                              start=False, stop=False)
                                    mm = pe.matmul(dst, w_lo[:, j, a:a + P], hidden_hi[buf][:, kb, cols],
                                                   start=False, stop=(kb == 1))
                                mm.then_inc(S["partial_full"], 1)
                                if half == 1 and j == 0:
                                    square_sums(norm, 2 * m)
                                    square_sums(norm, 2 * m + 1)
                    broadcast_rstd(norm, 0)
                    for j in range(KB, NSQ):
                        square_sums(norm, j)
                    broadcast_rstd(norm, 1)

                pair_by_halves(n0, o0, wait)
                hidden_panels(n0, o0, 2)
                with pe.Fori(0, (FFN_GROUPS - 1) // 2) as i:
                    for e in range(2):
                        hidden_panels(i * 12 + (n0 + 4 + 6 * e), i * 16 + (o0 + 8 + 8 * e))
                        out_panels(i * 12 + (n0 + 8 + 6 * e), i * 2 + e, e)
                last_out_panels(n0 + 6 * FFN_GROUPS - 2, FFN_GROUPS - 1, 0)

            out_projection(N_HGRN_OUT, O_HGRN_OUT, 1, 0, G_OUT)
            next_norm(2)
            ffn(0, N_FFN0, O_FFN0, start_wait(2, NSQ), 3)
            next_norm(4)

            def conv_block(blk, e, first=0):
                for j in range(first, 3):
                    gemm_panel(blk * 3 + (N_CONV + j), blk * 6 + (O_CONV + 2 * j), (e + j) % 2, (e + j) % 2)
                ada_sums(blk + G_CONV)

            pair_by_halves(N_CONV, O_CONV, start_wait(4, 2 * NSQ))
            conv_block(0, 0, 2)
            conv_block(1, 1)
            with pe.Fori(1, KB // 2) as i:
                conv_block(i * 2, 0)
                conv_block(i * 2 + 1, 1)
            out_projection(N_CONV_OUT, O_CONV_OUT, 5, NSQ)
            next_norm(6)
            ffn(1, N_FFN1, O_FFN1, start_wait(6, 3 * NSQ), 7)

        @block.scalar
        def _(act):
            def copy(dst, src, sem, func=ACT.Copy, **kw):
                nc.scalar.activation(dst, src, func, **kw).then_inc(S[sem], 1)

            def constants():
                act.wait_ge(S["consts"], 5)

            def square_step(norm, j, t):
                m, half = place(norm, j)
                if NSQ * norm + j >= 4:
                    act.wait_ge(S["squares_used"], NSQ * norm + j - 3)
                copy(squares[:, j % 4, :], t[:, m, cols_of(half)], "squares_ready", ACT.Square)

            def root(norm, half):
                c = slice(4 * half, 4 * half + 4)
                act.wait_ge(S["var_done"], 4 * norm + 2 * half + 2)
                copy(rstd[:, c], inv_var[:, c], "rstd_ready", ACT.Sqrt)

            for j in range(4):
                act.dma_start(ada_first[:, 4 * j:4 * j + 4, :],
                              ada_start[4 * j:4 * j + 4].rearrange("m p n -> p m n")
                              ).then_inc(S[f"ada_first{j}"], 16)
            act.sem_inc(S["gemm_evac"], 4)
            act.sem_inc(S["ctx_evac"], 1)
            for name in ("scan_evac", "o_squared"):
                act.sem_inc(S[name], credit[name])
            act.wait_ge(S["small_loaded"], 16 * 6)
            copy(silu_cond[:, :], cond_in[:, :], "silu_done", ACT.Silu)
            copy(lb_exp[:, 0:KB], lbr[:, :], "params", ACT.Copy)
            act.wait_ge(S["params"], 2)
            copy(lb_exp[:, KB:2 * KB], lb_exp[:, KB:2 * KB], "params", ACT.Exp)
            act.wait_ge(S["gates_done"], 1)
            for j in range(NSQ):
                if j % 4 == 0:
                    act.wait_ge(S["x_loaded"], 16 * (j // 4 + 1))
                square_step(0, j, xt)
            act.wait_ge(S["ctx_loaded"], 16)
            for part in range(2):
                act.wait_ge(S["squares_used"], NSQ - 2 + 2 * part)
                copy(squares[:, 2 * part:2 * part + 2, :].rearrange("p s (k t) -> p (s k) t", t=CTX),
                     ctxt[:, 4 * part:4 * part + 4, :], "csq_ready", ACT.Square)
            root(0, 0)
            root(0, 1)
            act.wait_ge(S["cvar_done"], 2)
            copy(crstd[:, :], cvar[:, CCH:2 * CCH], "crstd_ready", ACT.Sqrt)

            def residual_square(norm, sub, j):
                m, half = place(norm, j)
                act.wait_ge(S["x_updated"], updated(sub, m, half))
                square_step(norm, j, xt)

            def residual_squares(norm, sub):
                for j in range(KB + 4):
                    residual_square(norm, sub, j)
                    if j == KB - 1:
                        root(norm, 0)

            def modulate(norm, inst, scale, shift):
                for half in range(2):
                    for m in range(KB):
                        n = NSQ * inst + KB * half + m
                        act.wait_ge(S["scaled_done"], n + 1)
                        if n >= 4:
                            act.wait_ge(S["h_ready"], n - 3)
                        copy(modulated[:, m % 4, :], scaled[:, m % 4, :], "modulated_done", ACT.Identity,
                             scale=scale[:, m:m + 1], bias=shift[:, m:m + 1])
                        act.wait_ge(S["modulated_done"], n + 1)
                        copy(h_hi[:, m, cols_of(half)], modulated[:, m % 4, :], "h_hi_done")
                        if norm > 0 and half == 0 and m < 4:
                            residual_square(norm, inst - 1, KB + 4 + m)
                        if norm > 0 and half == 0 and m == KB - 1:
                            root(norm, 1)

            act.wait_ge(S["cmod_done"], 4)
            act.wait_ge(S["cscaled"], 1)
            modulate(0, 0, in_scale[:, 0:KB], mods[:, 0:KB])
            for m in range(KB):
                copy(ctxt[:, m, :], ctxt[:, m, :], "cmodulated", ACT.Identity,
                     scale=in_scale[:, 4 * KB + m:4 * KB + m + 1], bias=cmods[:, m:m + 1])
            act.wait_ge(S["cmodulated"], KB)
            copy(hc_hi[:, :, :], ctxt[:, :, :], "chi_done")

            def head(gemm_of, scan_of, parity):
                hg, hs = gemm_of, scan_of

                def evacuate(i, half, dst, **kw):
                    o = hg * 10 + (O_HEADS + 2 * i + half)
                    act.wait_ge(S["gemm_full"], o + 1)
                    copy(dst, bank(2 * ((parity + i) % 2) + half), "gemm_evac", **kw)

                def evacuate_ctx(ci, dst):
                    act.wait_ge(S["ctx_full"], hg * 3 + (ci + 1))
                    copy(dst, ctx_out, "ctx_evac")

                def cols(t, half, off=0):
                    return t[:, off + half * HALF:off + (half + 1) * HALF]

                def scan_bank(use):
                    act.wait_ge(S["scan_full"], hs * SCAN_USES + (SCAN_USES + use + 1))
                    return SCAN_BANKS[use % 2]

                def chunks_out(use, dst, n):
                    b = scan_bank(use)
                    copy(dst, bank(b, 0, n * P).rearrange("p (c t) -> p c t", t=P), "scan_evac")

                def key_tokens(d, part):
                    n = min(4, CHUNKS - 1 - 4 * part)
                    chunks_out((U_KF, U_KB)[d] + part, k_tok[:, 4 * part:4 * part + n, :], n)

                if hs is not None:
                    act.wait_ge(S["gemm_evac"], hs * 10 + (4 + O_HEADS + 4))
                    act.wait_ge(S["ctx_evac"], hs * 3 + 3)
                    act.wait_ge(S["scan_full"], hs * SCAN_USES + SCAN_USES)
                    for d in (FWD, BWD):
                        copy(gates[d][:, :], z[d][:, :], "sigmoids", ACT.Sigmoid)
                        copy(k[d][:, :], z[d][:, :], "sigmoids", ACT.Sigmoid, scale=-1.0)
                    for part in range(3):
                        n = min(4, CHUNKS - 4 * part)
                        chunks_out(U_V + part, v_tok[:, 4 * part:4 * part + n, :], n)
                    act.wait_ge(S["gemm_evac"], hs * 10 + (4 + O_HEADS + 10))
                    constants()
                    copy(mix[:, bass.ds(hs, 1), :], g[:, :].unsqueeze(1), "gate_sig", ACT.Sigmoid)
                if hg is not None:
                    for half in range(2):
                        evacuate(0, half, cols(z[FWD], half, CTX))
                    evacuate_ctx(0, z[FWD][:, 0:CTX])
                    for half in range(2):
                        evacuate(1, half, cols(z[BWD], half, CTX))
                    evacuate_ctx(1, z[BWD][:, 0:CTX])
                    if hs is not None:
                        act.wait_ge(S["scan_full"], hs * SCAN_USES + (SCAN_USES + U_DIAG + 2))
                        act.wait_ge(S["scan_b"], hs * 22 + 1)
                    for half in range(2):
                        evacuate(2, half, cols(q, half), scale=float(P) ** -0.5)
                if hs is not None:
                    for part in range(3):
                        key_tokens(FWD, part)
                    for part in range(3):
                        key_tokens(BWD, part)
                if hg is not None:
                    if hs is not None:
                        act.wait_ge(S["scan_full"], hs * SCAN_USES + (SCAN_USES + U_V + 3))
                    for half in range(2):
                        evacuate(3, half, cols(v_t, half, CTX))
                    evacuate_ctx(2, v_t[:, 0:CTX])
                if hs is not None:
                    for part in range(2):
                        b = scan_bank(U_O + part)
                        copy(cols(o_sq, part), bank(b), "o_squared", ACT.Square)
                    act.wait_ge(S["ovar_done"], hs * 2 + 2)
                    copy(orstd[:, :], ovar[:, LAT:2 * LAT], "orstd_ready", ACT.Sqrt)
                if hg is not None:
                    if hs is not None:
                        act.wait_ge(S["gs_ready"], hs + 1)
                    for half in range(2):
                        evacuate(4, half, cols(g, half))

            act.wait_ge(S["scaled_done"], NSQ)
            head(0, None, 0)
            act.wait_ge(S["hc_ready"], 1)
            with act.Fori(0, HEADS // 2 - 1) as i:
                head(i * 2 + 1, i * 2, 1)
                head(i * 2 + 2, i * 2 + 1, 0)
            head(HEADS - 1, HEADS - 2, 1)
            head(None, HEADS - 1, 0)

            def split_mix(before, ready, last_started):
                act.wait_ge(S["gemm_full"], last_started)
                for half in range(2):
                    for m in range(KB):
                        ready(m, half)
                        copy(h_hi[:, m, cols_of(half)], mix[:, m, cols_of(half)], "mix_hi")

            def out_projection(o0, norm):
                def out_half(m, half, pos):
                    act.wait_ge(S["gemm_full"], o0 + pos + 1)
                    copy(y[:, m, cols_of(half)], bank(pos % 4), "gemm_evac")

                def squares_of(m, half, pos):
                    act.wait_ge(S["gemm_evac"], 4 + o0 + pos + 1)
                    square_step(norm, 2 * m + half, y)

                for pos, (m, half) in enumerate(((0, 0), (1, 0), (0, 1), (1, 1))):
                    out_half(m, half, pos)
                for m, half, pos in ((0, 0, 0), (0, 1, 2), (1, 0, 1), (1, 1, 3)):
                    squares_of(m, half, pos)
                for m in range(2, KB):
                    for half in range(2):
                        out_half(m, half, 2 * m + half)
                        squares_of(m, half, 2 * m + half)
                        if m == KB - 1:
                            root(norm, half)

            def ffn(f, o0, norm):
                def hidden_block(blk, o, j):
                    for half in range(2):
                        act.wait_ge(S["hidden_done"], blk * 2 + (4 * FFN_GROUPS * f + half + 1))
                        act.wait_ge(S["gemm_full"], o + half + 1)
                        copy(gate_act[:, half, :], bank(half), "gemm_evac", ACT.Silu)
                    for half in range(2):
                        act.wait_ge(S["gemm_full"], o + 2 + half + 1)
                        copy(up_copy[:, half, :], bank(2 + half), "gemm_evac")

                act.wait_ge(S["h_ready"], NSQ * (2 + 2 * f))
                for half in range(2):
                    act.wait_ge(S["hidden_done"], 4 * FFN_GROUPS * f + half + 1)
                    act.wait_ge(S["gemm_full"], o0 + 2 * half + 1)
                    copy(gate_act[:, half, :], bank(2 * half), "gemm_evac", ACT.Silu)
                    act.wait_ge(S["gemm_full"], o0 + 2 * half + 2)
                    copy(up_copy[:, half, :], bank(2 * half + 1), "gemm_evac")
                with act.Fori(1, 2 * FFN_GROUPS) as i:
                    hidden_block(i, i * 4 + o0, 0)
                for j in range(NSQ):
                    act.wait_ge(S["partial_evac"], 4 + 16 * FFN_GROUPS * (f + 1) - 16 + j + 1)
                    square_step(norm, j, y)
                    if j % KB == KB - 1:
                        root(norm, j // KB)

            split_mix(0, lambda m, half: act.wait_ge(S["mix_ready"], credit["mix_ready"] + 2 * m + half + 1),
                      O_HGRN_OUT)
            out_projection(O_HGRN_OUT, 1)
            residual_squares(2, 0)
            act.wait_ge(S["mods_ready"], 2)
            modulate(2, 1, in_scale[:, KB:2 * KB], mods[:, 3 * KB:4 * KB])
            ffn(0, O_FFN0, 3)
            residual_squares(4, 1)
            act.wait_ge(S["mods_ready"], 4)
            modulate(4, 2, in_scale[:, 2 * KB:3 * KB], mods[:, 6 * KB:7 * KB])

            def conv_block(blk, e, first=0):
                for j, (dst, need) in list(enumerate(((conv_c, 1), (conv_x, 1), (conv_b, 5))))[first:]:
                    act.wait_ge(S["conv_done"], blk * 5 + need)
                    for half in range(2):
                        act.wait_ge(S["gemm_full"], blk * 6 + (O_CONV + 2 * j + half + 1))
                        copy(dst[:, half * HALF:(half + 1) * HALF], bank(2 * ((e + j) % 2) + half), "gemm_evac")

            act.wait_ge(S["conv_done"], 1)
            for pos in range(4):
                act.wait_ge(S["gemm_full"], O_CONV + pos + 1)
                copy((conv_c, conv_x)[pos % 2][:, cols_of(pos // 2)], bank(pos), "gemm_evac")
            conv_block(0, 0, 2)
            conv_block(1, 1)
            with act.Fori(1, KB // 2) as i:
                conv_block(i * 2, 0)
                conv_block(i * 2 + 1, 1)
            split_mix(NSQ, lambda m, half: act.wait_ge(S["conv_done"], 5 + 5 * m + 5), O_CONV_OUT)
            out_projection(O_CONV_OUT, 5)
            residual_squares(6, 2)
            act.wait_ge(S["mods_ready"], 6)
            modulate(6, 3, in_scale[:, 3 * KB:4 * KB], mods[:, 9 * KB:10 * KB])
            ffn(1, O_FFN1, 7)

        @block.vector
        def _(dve):
            V = nc.vector

            def tt(dst, a, b, op, sem):
                V.tensor_tensor(dst, a, b, op).then_inc(S[sem], 1)

            for name in ("scores_evac", "state_f", "state_b", "o_gated", "mix_ready"):
                dve.sem_inc(S[name], credit[name])
            dve.sem_inc(S["hidden_done"], 2)
            dve.sem_inc(S["partial_evac"], 4)
            dve.sem_inc(S["conv_done"], 5)

            dve.wait_ge(S["small_loaded"], 16 * 6)
            dve.wait_ge(S["params"], 1)
            one_layer = lb_exp[:, 0:KB]
            e = lb_exp[:, KB:2 * KB]
            inv = lb_exp[:, 2 * KB:3 * KB]
            tt(e, lbr[:, :], one_layer, ALU.subtract, "params")
            dve.wait_ge(S["masks_f32"], 4 * LEVELS)
            V.tensor_copy(masks[:, :, :], mask_f32[:, :, :]).then_inc(S["gates_done"], 1)
            dve.wait_ge(S["params"], 3)
            V.reciprocal(inv, e).then_inc(S["params"], 1)
            dve.wait_ge(S["params"], 4)
            tt(e, e, inv, ALU.mult, "params")
            dve.wait_ge(S["params"], 5)
            tt(lb[:, :], e, e, ALU.subtract, "params")
            dve.wait_ge(S["params"], 6)
            V.tensor_scalar(one_minus_lb[:, :], lb[:, :], -1.0, 1.0, ALU.mult, ALU.add).then_inc(S["params"], 1)
            dve.wait_ge(S["params"], 7)
            dve.wait_ge(S["gates_done"], 1)

            def variance(norm, half):
                c = slice(4 * half, 4 * half + 4)
                last = NSQ - 1 + half if norm in BY_BLOCK else KB * (half + 1)
                dve.wait_ge(S["squares_used"], NSQ * norm + (last if norm > 0 else NSQ))
                V.tensor_scalar(var[:, c], sum_out[norm][:, c], 1.0 / D, EPS, ALU.mult, ALU.add
                                ).then_inc(S["var_done"], 1)
                dve.wait_ge(S["var_done"], 4 * norm + 2 * half + 1)
                V.reciprocal(inv_var[:, c], var[:, c]).then_inc(S["var_done"], 1)

            def make_h(norm, inst):
                def low(half, m):
                    dve.wait_ge(S["h_hi_done"], NSQ * inst + KB * half + m + 1)
                    tt(h_lo[:, m, cols_of(half)], modulated[:, m % 4, :], h_hi[:, m, cols_of(half)],
                       ALU.subtract, "h_ready")

                for half in range(2):
                    dve.wait_ge(S["bc_full"], 2 * norm + half + 1)
                    for m in range(KB):
                        n = NSQ * inst + KB * half + m
                        if n >= 4:
                            dve.wait_ge(S["modulated_done"], n - 3)
                        tt(scaled[:, m % 4, :], xt[:, m, cols_of(half)], bank(bc(norm, half)), ALU.mult, "scaled_done")
                        if m >= 2:
                            low(half, m - 2)
                    low(half, KB - 2)
                    low(half, KB - 1)
                    if norm > 0 and half == 0:
                        variance(norm, 1)

            def add_residual(norm, sub):
                for half in range(2):
                    dve.wait_ge(S["bc_full"], 2 * norm + half + 1)
                    n0 = 2 * KB * (2 * sub + half)
                    cols = cols_of(half)
                    for m in range(KB + 1):
                        if m < KB:
                            tt(y[:, m, cols], y[:, m, cols], bank(bc(norm, half)), ALU.mult, "x_updated")
                        if m == 0:
                            continue
                        r = m - 1
                        dve.wait_ge(S["x_updated"], n0 + (2 * r + 1 if r == 0 else 2 * r))
                        V.scalar_tensor_tensor(xt[:, r, cols], y[:, r, cols],
                                               out_scale[:, sub * KB + r:sub * KB + r + 1],
                                               xt[:, r, cols], ALU.mult, ALU.add).then_inc(S["x_updated"], 1)
                        if m == 2 and half == 0:
                            variance(norm, 1)
                        if m == 7 and half == 1 and norm < 7:
                            variance(norm + 1, 0)

            variance(0, 0)
            variance(0, 1)
            dve.wait_ge(S["csq_used"], 2)
            V.tensor_scalar(cvar[:, 0:CCH], csum_out, 1.0 / D, EPS, ALU.mult, ALU.add).then_inc(S["cvar_done"], 1)
            dve.wait_ge(S["cvar_done"], 1)
            V.reciprocal(cvar[:, CCH:2 * CCH], cvar[:, 0:CCH]).then_inc(S["cvar_done"], 1)
            dve.wait_ge(S["cbc_full"], 1)
            tt(ctxt[:, :, :], ctxt[:, :, :], bank(7, 0, CTX).unsqueeze(1).broadcast_to([P, KB, CTX]),
               ALU.mult, "cscaled")
            dve.wait_ge(S["ada_first_done"], 1)
            sums = ada_first_out.rearrange("p (m two) -> p two m", two=2)
            tt(mods[:, 0:2 * KB], sums[:, 0, :], bias[:, 0:2 * KB], ALU.add, "cmod_done")
            tt(cmods[:, :], sums[:, 1, :], bias[:, 0:2 * KB], ALU.add, "cmod_done")
            dve.wait_ge(S["cmod_done"], 2)

            def weigh(dst, scale, weights, sem):
                V.scalar_tensor_tensor(dst, scale, 1.0, weights, ALU.add, ALU.mult).then_inc(S[sem], 1)

            weigh(in_scale[:, 0:KB], mods[:, KB:2 * KB], nw[:, 0:KB], "cmod_done")
            weigh(in_scale[:, 4 * KB:5 * KB], cmods[:, KB:2 * KB], nw[:, 0:KB], "cmod_done")
            make_h(0, 0)
            dve.wait_ge(S["chi_done"], 1)
            tt(hc_lo[:, :, :], ctxt[:, :, :], hc_hi[:, :, :], ALU.subtract, "hc_ready")

            def ada_rows(g, a):
                dve.wait_ge(S[f"ada_loaded{a % 2}"], g * 32 + 16 * (a // 2 + 1))
                for t in range(2):
                    kb = 2 * a + t
                    src = ada_raw[:, a % 2, t * HALF:(t + 1) * HALF]
                    weight = silu_cond[:, 2 * kb:2 * kb + 1]
                    if kb == 0:
                        dve.wait_ge(S["ada_summed"], g + 1)
                        V.tensor_scalar(ada_acc[:, :], src, weight, None, ALU.mult).then_inc(S["ada_step"], 1)
                    else:
                        dve.wait_ge(S["ada_step"], g * 8 + kb)
                        V.scalar_tensor_tensor(ada_acc[:, :], src, weight, ada_acc[:, :],
                                               ALU.mult, ALU.add).then_inc(S["ada_step"], 1)

            def ada_bias_add(g):
                dve.wait_ge(S["ada_summed"], g + 2)
                cols = bass.ds(g * ADA_GROUP + ADA_START, ADA_GROUP)
                tt(mods[:, cols], ada_out, bias[:, cols], ALU.add, "ada_evac")

            def head(gemm_of, scan_of):
                hg, hs = gemm_of, scan_of

                def scan_bank(use):
                    dve.wait_ge(S["scan_full"], hs * SCAN_USES + (SCAN_USES + use + 1))
                    return SCAN_BANKS[use % 2]

                def q_and_totals(d):
                    V.tensor_tensor(qd[d][:, :], q[:, :], lat(gates[d]), ALU.mult).then_inc(scan_sem[d], 1)

                def decay_level(i, d):
                    b, n = 1 << i, ALL >> (i + 1)
                    use = scan_bank(U_LEVEL + 2 * i + d)
                    tot = total_of(d, i).rearrange("p (n two) -> p n two", two=2)
                    dve.wait_ge(scan_sem[d], hs * 22 + (1 + 3 * i))
                    kk = halves(k[d][:, :], b)[:, :, K_HALF[d], :]
                    V.tensor_tensor(kk, kk, tot[:, :, 1 - K_HALF[d]:2 - K_HALF[d]].broadcast_to([P, n, b]),
                                    ALU.mult).then_inc(scan_sem[d], 1)
                    nl = SEQ >> (i + 1)
                    qq = halves(qd[d][:, :], b)[:, :, Q_HALF[d], :]
                    V.tensor_tensor(qq, qq,
                                    tot[:, n - nl:, 1 - Q_HALF[d]:2 - Q_HALF[d]].broadcast_to([P, nl, b]),
                                    ALU.mult).then_inc(scan_sem[d], 1)
                    dve.wait_ge(S["scores_evac"], hs * SCORE_EVACS + (SCORE_EVACS + 2 + 2 * i + d))
                    V.tensor_tensor(total_of(d, i + 1), tot[:, :, 0], tot[:, :, 1], ALU.mult
                                    ).then_inc(scan_sem[d], 1)
                    dst = halves(scores[:, :, :].rearrange("p c t -> p (c t)"), b)[:, :, Q_HALF[d], :]
                    m = masks[:, d * LEVELS + i, :].unsqueeze(1).broadcast_to([P, LAT, P // 2])
                    V.copy_predicated(dst, m, bank(use)).then_inc(S["scores_evac"], 1)

                def states(d, part):
                    order = state_chunks(d)
                    for j in range(4 * part, min(4 * part + 4, CHUNKS - 1)):
                        if j % 4 == 0:
                            use = scan_bank((U_KVF, U_KVB)[d] + part)
                        src = bank(use, (j % 4) * P, (j % 4 + 1) * P)
                        step = -1 if d == BWD else 1
                        first = 0 if d == FWD else LAT - 1

                        def place(s):
                            return state[d][:, first + step * (1 if s == 1 else s - 2), :]

                        if j == 0:
                            dve.wait_ge(scan_sem[d], hs * 22 + 22)
                            V.tensor_copy(place(1), src).then_inc(state_sem[d], 1)
                        else:
                            dve.wait_ge(state_sem[d], hs * STATE_OPS + (STATE_OPS + j))
                            c = order[j]
                            V.scalar_tensor_tensor(place(j + 1), place(j), total_of(d, LEVELS)[:, c:c + 1], src,
                                                   ALU.mult, ALU.add).then_inc(state_sem[d], 1)

                if hs is not None:
                    lbs, oml = lb[:, bass.ds(hs, 1)], one_minus_lb[:, bass.ds(hs, 1)]
                    base_g = hs * 6 + 1
                    for d in (FWD, BWD):
                        dve.wait_ge(S["sigmoids"], hs * 4 + (2 * d + 1))
                        V.tensor_scalar(gates[d][:, :], gates[d][:, :], oml, lbs, ALU.mult, ALU.add
                                        ).then_inc(S["gates_done"], 1)
                        dve.wait_ge(S["sigmoids"], hs * 4 + (2 * d + 2))
                        V.tensor_scalar(k[d][:, :], k[d][:, :], oml, None, ALU.mult).then_inc(S["gates_done"], 1)
                        dve.wait_ge(S["gates_done"], base_g + (3 * d + 1))
                        V.tensor_scalar(gates[d][:, :], gates[d][:, :], F_FLOOR, None, ALU.max
                                        ).then_inc(S["gates_done"], 1)
                    dve.wait_ge(S["gates_done"], base_g + 6)
                    tt(k_sum[:, :], lat(k[FWD]), lat(k[BWD]), ALU.add, "diag_ready")
                    q_and_totals(FWD)
                    q_and_totals(BWD)
                    own = mix[:, bass.ds(hs, 1), :]
                    dve.wait_ge(S["gate_sig"], hs + 1)
                    tt(own, own, g[:, :].unsqueeze(1), ALU.mult, "gs_ready")
                    for part in range(2):
                        use = scan_bank(U_DIAG + part)
                        tt(scores[:, 4 * part:4 * part + 4, :], bank(use).rearrange("p (c t) -> p c t", t=P),
                           ident[:, :].unsqueeze(1).broadcast_to([P, 4, P]), ALU.mult, "scores_evac")
                    for i in range(LEVELS):
                        for d in (FWD, BWD):
                            decay_level(i, d)
                        if hg is not None and i == 3:
                            for a in range(2):
                                ada_rows(hg, a)
                    for d in (FWD, BWD):
                        for part in range(3):
                            states(d, part)
                    if hg is not None:
                        for a in range(2, ADA_GROUP):
                            ada_rows(hg, a)
                    dve.wait_ge(S["gs_ready"], hs + 1)
                    for part in range(2):
                        use = scan_bank(U_O + part)
                        half = own[:, :, part * HALF:(part + 1) * HALF]
                        dve.wait_ge(S["o_squared"], hs * 2 + (credit["o_squared"] + part + 1))
                        tt(half, bank(use).unsqueeze(1), half, ALU.mult, "o_gated")
                    dve.wait_ge(S["o_sum_full"], hs + 1)
                    V.tensor_scalar(ovar[:, 0:LAT], o_sum_out, 1.0 / P, EPS, ALU.mult, ALU.add
                                    ).then_inc(S["ovar_done"], 1)
                    dve.wait_ge(S["ovar_done"], hs * 2 + 1)
                    V.reciprocal(ovar[:, LAT:2 * LAT], ovar[:, 0:LAT]).then_inc(S["ovar_done"], 1)
                    for part in range(2):
                        use = scan_bank(U_BC + part)
                        half = own[:, :, part * HALF:(part + 1) * HALF]
                        V.scalar_tensor_tensor(half, half, gn[:, 0:1], bank(use).unsqueeze(1), ALU.mult, ALU.mult
                                               ).then_inc(S["mix_ready"], 1)
                elif hg is not None:
                    for a in range(ADA_GROUP):
                        ada_rows(hg, a)
                if hg is not None:
                    ada_bias_add(hg)

            dve.wait_ge(S["silu_done"], 1)
            head(0, None)
            with dve.Fori(0, HEADS // 2 - 1) as i:
                head(i * 2 + 1, i * 2)
                head(i * 2 + 2, i * 2 + 1)
            head(HEADS - 1, HEADS - 2)
            head(None, HEADS - 1)

            dve.wait_ge(S["ada_evac"], HEADS)
            tt(out_scale[:, 0:KB], mods[:, 2 * KB:3 * KB], nw[:, KB:2 * KB], ALU.mult, "mods_ready")
            weigh(in_scale[:, KB:2 * KB], mods[:, 4 * KB:5 * KB], nw[:, 2 * KB:3 * KB], "mods_ready")
            tt(out_scale[:, KB:2 * KB], mods[:, 5 * KB:6 * KB], nw[:, 3 * KB:4 * KB], ALU.mult, "mods_ready")

            def split_mix(inst):
                for half in range(2):
                    for m in range(KB):
                        dve.wait_ge(S["mix_hi"], NSQ * inst + KB * half + m + 1)
                        tt(h_lo[:, m, cols_of(half)], mix[:, m, cols_of(half)], h_hi[:, m, cols_of(half)],
                           ALU.subtract, "mix_split")

            def ffn(f):
                V.memset(y[:, :, :], 0.0).then_inc(S["y_zeroed"], 1)

                def hidden_block(blk, o, buf, kb, by_halves=False):
                    for half in range(2):
                        cols = slice(half * HALF, (half + 1) * HALF)
                        done = blk * 2 + (4 * FFN_GROUPS * f + half)
                        dve.wait_ge(S["gemm_evac"], o + (4 + (2 * half + 2 if by_halves else half + 3)))
                        tt(hidden[:, half, :], gate_act[:, half, :], up_copy[:, half, :], ALU.mult, "hidden_done")
                        dve.wait_ge(S["hidden_done"], done + 3)
                        V.tensor_copy(hidden_hi[buf][:, kb, cols], hidden[:, half, :]
                                      ).then_inc(S["hidden_hi_done"], 1)
                        dve.wait_ge(S["hidden_hi_done"], done + 1)
                        tt(hidden_lo[buf][:, kb, cols], hidden[:, half, :], hidden_hi[buf][:, kb, cols],
                           ALU.subtract, "hidden_ready")

                def add_last_partials(norm):
                    g0 = 16 * FFN_GROUPS * f + 16 * (FFN_GROUPS - 1)
                    dve.wait_ge(S["partial_evac"], g0 + 4)
                    for idx in range(NSQ):
                        m, half = idx % KB, idx // KB
                        dve.wait_ge(S["partial_full"], g0 + idx + 1)
                        tt(y[:, m, cols_of(half)], y[:, m, cols_of(half)], bank(4 + idx % 4), ALU.add,
                           "partial_evac")
                        if idx == KB + 3:
                            variance(norm, 0)

                def add_partials(grp):
                    g0 = 16 * FFN_GROUPS * f
                    dve.wait_ge(S["partial_evac"], grp * 16 + (g0 + 4))
                    for m in range(KB):
                        for half in range(2):
                            idx = 2 * m + half
                            dst = y[:, m, half * HALF:(half + 1) * HALF]
                            dve.wait_ge(S["partial_full"], grp * 16 + (g0 + idx + 1))
                            tt(dst, dst, bank(4 + idx % 4), ALU.add, "partial_evac")

                def hidden_group(grp, o, buf, first=False):
                    for kb in range(2):
                        hidden_block(grp * 2 + kb, o + 4 * kb, buf, kb, first and kb == 0)

                o0 = (O_FFN0, O_FFN1)[f]
                hidden_group(0, o0, 0, first=True)
                dve.wait_ge(S["y_zeroed"], f + 1)
                with dve.Fori(0, (FFN_GROUPS - 1) // 2) as i:
                    for e in range(2):
                        hidden_group(i * 2 + (e + 1), i * 16 + (o0 + 8 + 8 * e), 1 - e)
                        add_partials(i * 2 + e)
                add_last_partials(AFTER_FFN[f])

            split_mix(0)
            for group in range(G_OUT, G_CONV):
                for a in range(ADA_GROUP):
                    ada_rows(group, a)
                ada_bias_add(group)
            dve.wait_ge(S["ada_evac"], G_CONV)
            weigh(in_scale[:, 2 * KB:3 * KB], mods[:, 7 * KB:8 * KB], nw[:, 4 * KB:5 * KB], "mods_ready")
            variance(1, 0)
            dve.wait_ge(S["x_reloaded"], 16)
            dve.wait_ge(S["mods_ready"], 4)
            add_residual(1, 0)
            make_h(2, 1)
            ffn(0)
            add_residual(3, 1)
            make_h(4, 2)

            def conv_block(blk):
                rows = SEQ // GRID_W
                u = conv_u[:, :].rearrange("p (r w) -> p r w", w=GRID_W)
                v = conv_v[:, :].rearrange("p (r w) -> p r w", w=GRID_W)
                own = mix[:, bass.ds(blk, 1), :]

                def tap(j):
                    return cw[:, bass.ds(blk + j * KB, 1)]

                for a in range(ADA_GROUP):
                    ada_rows(blk + G_CONV, a)
                c0 = blk * 5 + 5
                dve.wait_ge(S["gemm_evac"], blk * 6 + (4 + O_CONV + 4))
                tt(conv_u[:, :], conv_c[:, :], conv_x[:, :], ALU.mult, "conv_done")
                dve.wait_ge(S["conv_done"], c0 + 1)
                V.tensor_scalar(conv_v[:, :], conv_u[:, :], tap(1), None, ALU.mult).then_inc(S["conv_done"], 1)
                dve.wait_ge(S["conv_done"], c0 + 2)
                V.scalar_tensor_tensor(v[:, :, 1:], u[:, :, :GRID_W - 1], tap(0), v[:, :, 1:],
                                       ALU.mult, ALU.add).then_inc(S["conv_done"], 1)
                dve.wait_ge(S["conv_done"], c0 + 3)
                V.scalar_tensor_tensor(v[:, :, :GRID_W - 1], u[:, :, 1:], tap(2), v[:, :, :GRID_W - 1],
                                       ALU.mult, ALU.add).then_inc(S["conv_done"], 1)
                dve.wait_ge(S["gemm_evac"], blk * 6 + (4 + O_CONV + 6))
                dve.wait_ge(S["conv_done"], c0 + 4)
                tt(own, conv_v[:, :].unsqueeze(1), conv_b[:, :].unsqueeze(1), ALU.mult, "conv_done")
                ada_bias_add(blk + G_CONV)

            with dve.Fori(0, KB) as i:
                conv_block(i)
            dve.wait_ge(S["ada_evac"], G_CONV + KB)
            tt(out_scale[:, 2 * KB:3 * KB], mods[:, 8 * KB:9 * KB], nw[:, 5 * KB:6 * KB], ALU.mult, "mods_ready")
            weigh(in_scale[:, 3 * KB:4 * KB], mods[:, 10 * KB:11 * KB], nw[:, 6 * KB:7 * KB], "mods_ready")
            tt(out_scale[:, 3 * KB:4 * KB], mods[:, 11 * KB:12 * KB], nw[:, 7 * KB:8 * KB], ALU.mult, "mods_ready")
            split_mix(1)
            variance(5, 0)
            dve.wait_ge(S["mods_ready"], 7)
            add_residual(5, 2)
            make_h(6, 3)
            ffn(1)
            add_residual(7, 3)


def kernel(x, c, ctx, c_ctx, ada_w, ada_b, norm_w, hgrn_w_in, hgrn_w_out, hgrn_gnorm, hgrn_lb,
           conv_w_in, conv_w, conv_w_out, ffn_w_in, ffn_w_out):
    import numpy as np
    import concourse.bacc as bacc
    from concourse.bass_utils import run_bass_kernel_spmd

    a = np.asarray

    def panels(w, parts=1):
        kb, m = w.shape[0] // P, w.shape[1] // parts // P
        return w.reshape(kb, P, parts, m, P).transpose(3, 2, 1, 0, 4)

    def channels(v):
        return a(v).reshape(-1, KB, P).transpose(2, 0, 1).reshape(P, -1)

    arrays = {}
    arrays["x"] = a(x)[0].T.reshape(KB, P, SEQ)
    arrays["ctx"] = a(ctx)[0].T.reshape(KB, P, CTX)
    arrays["cond"] = np.stack([a(c)[0], a(c_ctx)]).reshape(2, KB, P).transpose(2, 1, 0).reshape(P, 2 * KB)
    ada_first = panels(a(ada_w)[0])[:ADA_START, 0]
    arrays["ada_start"] = ada_first.reshape(ADA_START, P, D)
    arrays["ada"] = np.concatenate([w.reshape(ADA_GROUP, 2, P, -1, HALF).transpose(3, 0, 2, 1, 4).reshape(-1, P, D)
                                    for w in a(ada_w)])[ADA_START:]
    arrays["ada_bias"] = channels(ada_b)
    arrays["norm_w"] = channels(norm_w)
    arrays["lb_raw"] = channels(hgrn_lb)
    arrays["gnorm"] = a(hgrn_gnorm).reshape(P, 1)
    arrays["conv_w"] = channels(conv_w)
    arrays["w_hgrn_in"] = panels(a(hgrn_w_in)[0], 5)[:, list(HEAD_PARTS)].reshape(-1, P, D)
    arrays["w_hgrn_out"] = panels(a(hgrn_w_out)[0]).reshape(-1, P, D)
    arrays["w_conv_in"] = panels(a(conv_w_in)[0], 3)[:, [1, 2, 0]].reshape(-1, P, D)
    arrays["w_conv_out"] = panels(a(conv_w_out)[0]).reshape(-1, P, D)
    arrays["w_ffn_in"] = np.stack([panels(w, 2).reshape(-1, P, D) for w in a(ffn_w_in)])
    arrays["w_ffn_out"] = a(ffn_w_out).reshape(2, FFN_GROUPS, 2, P, 2, 4, P).transpose(
        0, 1, 4, 3, 2, 5, 6).reshape(2, 2 * FFN_GROUPS, P, D)
    arrays = {n: np.ascontiguousarray(v) for n, v in arrays.items()}

    nc = bacc.Bacc("TRN2", target_bir_lowering=False, num_devices=1, dynamic_dma_scratch_size=1024)
    aps = {n: nc.dram_tensor("in_" + n, v.shape, mybir.dt.from_np(v.dtype), kind="ExternalInput").ap()
           for n, v in arrays.items()}
    out = nc.dram_tensor("out", (KB, P, SEQ), F32, kind="ExternalOutput").ap()
    build_trunk(nc, out=out, **aps)
    r = run_bass_kernel_spmd(nc, [{"in_" + n: v for n, v in arrays.items()}], core_ids=[0])
    return r.results[0]["out"].reshape(D, SEQ).T.reshape(1, SEQ, D)
```

```python
from contextlib import ExitStack

import concourse.bass as bass
from concourse import mybir

F32 = mybir.dt.float32
F32R = mybir.dt.float32r
U8 = mybir.dt.uint8
ACT = mybir.ActivationFunctionType
ALU = mybir.AluOpType

P = 128
D = 1024
KB = D // P
SEQ, CTX = 1024, 256
HALF = 512
GRID_W = 64
HEADS = D // P
FFN = 2816
FFN_GROUPS = FFN // (2 * P)
LAT = SEQ // P
CCH = CTX // P
CHUNKS = CCH + LAT
ALL = CHUNKS * P
LEVELS = 7
EPS = 1e-6
F_FLOOR = 1e-6
FWD, BWD = 0, 1
HEAD_PARTS = (2, 3, 0, 1, 4)
HEAD_PANELS = len(HEAD_PARTS)
ADA_START = 16
ADA_GROUP = 4
G_OUT = HEADS
G_CONV = G_OUT + 4
FFN_HIDDEN_PANELS, FFN_OUT_PANELS = 4, 2

HEAD_ADA = ((), (0, 1), (), (2, 3), ())
CONV_ADA = ((0, 1), (2,), (3,))

N_HEADS = 0
N_HGRN_OUT = N_HEADS + HEADS * HEAD_PANELS
N_FFN0 = N_HGRN_OUT + KB
N_CONV = N_FFN0 + FFN_GROUPS * 6
N_CONV_OUT = N_CONV + KB * 3
N_FFN1 = N_CONV_OUT + KB
N_PANELS = N_FFN1 + FFN_GROUPS * 6
O_HEADS = 0
O_HGRN_OUT = O_HEADS + 2 * HEADS * HEAD_PANELS
O_FFN0 = O_HGRN_OUT + 2 * KB
O_CONV = O_FFN0 + 8 * FFN_GROUPS
O_CONV_OUT = O_CONV + 6 * KB
O_FFN1 = O_CONV_OUT + 2 * KB

SCAN_BANKS = (4, 5)
U_V, U_DIAG, U_LEVEL, U_KF, U_KVF, U_KB, U_KVB, U_O, U_BC = 0, 3, 5, 19, 22, 25, 28, 31, 33
SCAN_USES = 35
ACT_EVACS = 9
NSQ = 2 * KB
BY_BLOCK = (0, 1, 5)
AFTER_FFN = (3, 7)
SCORE_EVACS = 16
STATE_OPS = 9
SCAN_STEPS = 1 + 5 * LEVELS
STATE_AT = (4, 8, 9)


def scan_readers(use):
    if use < U_DIAG:
        return [("scan_evac", ACT_EVACS, use)]
    if use < U_KF:
        return [("scores_evac", SCORE_EVACS, use - U_DIAG)]
    if use < U_KVF:
        return [("scan_evac", ACT_EVACS, 3 + use - U_KF)]
    if use < U_KB:
        return [("state_f", STATE_OPS, STATE_AT[use - U_KVF] - 1)]
    if use < U_KVB:
        return [("scan_evac", ACT_EVACS, 6 + use - U_KB)]
    if use < U_O:
        return [("state_b", STATE_OPS, STATE_AT[use - U_KVB] - 1)]
    if use < U_BC:
        return [("o_gated", 2, use - U_O)]
    return [("mix_ready", 2, use - U_BC)]


def updated(sub, m, half):
    return 2 * KB * (2 * sub + half) + min(2 * m + 3, 2 * KB)


def early(half, m):
    return (KB - 1) * half + m if m < KB - 1 else 2 * (KB - 1) + half


def added(norm, half):
    return NSQ * norm + (NSQ - 1 + half if norm in BY_BLOCK else KB * (half + 1))


def place(norm, j):
    return (j // 2, j % 2) if norm in BY_BLOCK else (j % KB, j // KB)


def pick(t, i):
    return t[i] if isinstance(i, int) else t[bass.ds(i, 1)].rearrange("o p n -> (o p) n")


def state_chunks(d):
    if d == FWD:
        return list(range(CHUNKS - 1))
    return list(range(CCH - 1, -1, -1)) + list(range(CHUNKS - 1, CCH, -1))


def build_trunk(nc, x, ctx, cond, ada, ada_bias, norm_w, lb_raw, gnorm, conv_w,
                w_hgrn_in, w_hgrn_out, w_conv_in, w_conv_out, w_ffn_in, w_ffn_out, out):
    base = (nc.sbuf_base + 31) // 32 * 32

    def at(name, kib, shape, dt=F32):
        return nc.alloc_sbuf_tensor_at(name, shape, dt, offset=base + int(kib * 1024))

    h_hi = at("h_hi", 0, [P, KB, SEQ], F32R)
    h_lo = at("h_lo", 32, [P, KB, SEQ], F32R)
    ada_first = at("ada_first", 0, [P, ADA_START, D])
    start_acc = at("start_acc", 184, [P, 2, ADA_START // ADA_GROUP, HALF])
    mix = at("mix", 64, [P, KB, SEQ])
    y = at("y", 64, [P, KB, SEQ])
    w_raw = at("w_raw", 96, [P, 2, D])
    w_hi = at("w_hi", 104, [P, 2, D], F32R)
    w_lo = at("w_lo", 112, [P, 2, D], F32R)
    ada_raw = at("ada_raw", 120, [P, 2, D])
    xt = at("xt", 128, [P, KB, SEQ])
    hc_hi = at("hc_hi", 160, [P, KB, CTX], F32R)
    hc_lo = at("hc_lo", 168, [P, KB, CTX], F32R)
    ctxt = at("ctxt", 176, [P, KB, CTX])
    scaled = at("scaled", 184, [P, 4, HALF])
    modulated = at("modulated", 192, [P, 4, HALF])
    squares = at("squares", 204, [P, 4, HALF])
    hidden_hi = [at(f"hidden_hi{i}", 160 + 16 * i, [P, 2, SEQ], F32R) for i in range(2)]
    hidden_lo = [at(f"hidden_lo{i}", 168 + 16 * i, [P, 2, SEQ], F32R) for i in range(2)]
    gate_act = at("gate_act", 192, [P, 2, HALF])
    up_copy = at("up_copy", 196, [P, 2, HALF])
    hidden = at("hidden", 200, [P, 2, HALF])
    conv_u = at("conv_u", 160, [P, SEQ])
    conv_v = at("conv_v", 164, [P, SEQ])
    conv_c = at("conv_c", 168, [P, SEQ])
    conv_x = at("conv_x", 172, [P, SEQ])
    conv_b = at("conv_b", 176, [P, SEQ])
    z = [at("z_f", 128, [P, ALL]), at("z_b", 133, [P, ALL])]
    q = at("q", 138, [P, SEQ])
    g = at("g", 142, [P, SEQ])
    v_t = at("v_t", 146, [P, ALL])
    v_tok = at("v_tok", 151, [P, CHUNKS, P])
    scores = at("scores", 156, [P, LAT, P])
    gates = [at("gates_f", 176, [P, ALL]), at("gates_b", 181, [P, ALL])]
    k_all = at("k_all", 186, [P, 2, ALL])
    q_all = at("q_all", 196, [P, 2, SEQ])
    k = [k_all[:, 0, :], k_all[:, 1, :]]
    qd = [q_all[:, 1, :], q_all[:, 0, :]]
    totals = [at("totals_f", 204, [P, ALL // 2]), at("totals_b", 206.5, [P, ALL // 2])]
    k_sum = at("k_sum", 209, [P, SEQ])
    k_both = at("k_both", 209, [P, SEQ])
    k_tok = at("k_tok", 209, [P, CHUNKS - 1, P])
    o_sq = at("o_sq", 209, [P, SEQ])
    totals_even = [at("totals_even_f", 176, [P, ALL // 4]), at("totals_even_b", 181, [P, ALL // 4])]
    state = [at("state_f_t", 176, [P, LAT, P]), at("state_b_t", 181, [P, LAT, P])]
    ident = at("ident", 214, [P, P])
    masks = at("masks", 214.5, [P, LEVELS, P], U8)
    mask_f32 = at("mask_f32", 204, [P, LEVELS, P])
    small_at = [215.5]

    def small(name, n):
        t = at(name, small_at[0], [P, n])
        small_at[0] += (4 * n + 31) // 32 * 32 / 1024
        return t

    ones = small("ones", 1)
    zero = small("zero", 1)
    cond_in = small("cond_in", 2 * KB)
    silu_cond = small("silu_cond", 2 * KB)
    bias = small("bias", 12 * KB)
    mods = small("mods", 12 * KB)
    cmods = small("cmods", 2 * KB)
    nw = small("nw", 8 * KB)
    lbr = small("lbr", KB)
    lb_exp = small("lb_exp", 3 * KB)
    lb = small("lb", KB)
    one_minus_lb = small("one_minus_lb", KB)
    gn = small("gn", 1)
    cw = small("cw", 3 * KB)
    in_scale = small("in_scale", 5 * KB)
    out_scale = small("out_scale", 4 * KB)
    var = small("var", KB)
    inv_var = small("inv_var", KB)
    rstd = small("rstd", KB)
    cvar = small("cvar", 2 * CCH)
    crstd = small("crstd", CCH)
    ada_acc = small("ada_acc", HALF)
    square_acc = [at("square_acc0", 212, [P, HALF]), small("square_acc1", HALF)]
    ovar = small("ovar", 2 * LAT)
    orstd = small("orstd", LAT)
    assert base + (small_at[0]) * 1024 <= nc.sbuf_usable_end

    ctx_mgr = ExitStack()
    with ctx_mgr:
        psum = ctx_mgr.enter_context(nc.psum_tensor("psum", [P, 8 * HALF], F32))
        names = """panel_loaded0 panel_loaded1 w_hi_done panel_split panel_started
            gemm_full gemm_evac ctx_full ctx_evac
            ada_first0 ada_first1 ada_first2 ada_first3 start_step ada_loaded0 ada_loaded1 ada_step ada_first_done ada_summed ada_evac
            small_loaded x_loaded0 x_loaded1 x_loaded2 x_loaded3 ctx_loaded x_reloaded stored
            masks_f32 consts silu_done cmod_done params
            squares_ready squares_used summed var_done rstd_ready bc_full scaled_done x_updated
            modulated_done h_hi_done h_ready
            csq_ready csq_used cvar_done crstd_ready cbc_full cscaled cmodulated chi_done hc_ready
            sigmoids gates_done diag_ready scan_f scan_b k_merged scan_full scan_evac scores_evac state_f state_b
            gate_sig gs_ready o_squared o_gated o_sum_full ovar_done orstd_ready mix_ready mods_ready
            mix_hi mix_split
            hidden_done hidden_hi_done hidden_ready partial_full partial_evac y_zeroed
            conv_done""".split()
        S = {n: ctx_mgr.enter_context(nc.semaphore(n)) for n in names}
        scan_sem = [S["scan_f"], S["scan_b"]]
        state_sem = [S["state_f"], S["state_b"]]
        credit = {n: c for n, c in (("scan_evac", ACT_EVACS), ("scores_evac", SCORE_EVACS),
                                    ("state_f", STATE_OPS), ("state_b", STATE_OPS), ("o_squared", 2),
                                    ("o_gated", 2), ("mix_ready", 2))}

        def bank(i, a=0, b=HALF):
            return psum[:, i * HALF + a:i * HALF + b]

        csum_out = bank(2, 0, CCH)
        ada_first_out = bank(3, 0, 2 * ADA_START)
        ctx_out = bank(6, 0, CTX)
        sum_out = [bank(0 if norm in AFTER_FFN else 6, 0, KB) for norm in range(8)]
        ada_out = bank(7, 0, ADA_GROUP)
        o_sum_out = bank(7, 64, 64 + LAT)

        def bc(norm, half):
            return (2 if norm in AFTER_FFN else 4) + half

        def chunk(t, c):
            return t[:, c * P:(c + 1) * P]

        def cols_of(half):
            return slice(half * HALF, (half + 1) * HALF)

        def lat(t):
            return t[:, CTX:ALL]

        def halves(ap, b):
            return ap.rearrange("p (n two b) -> p n two b", two=2, b=b)

        def both(t, first, b):
            one = t[:, 0, first:first + P]
            width = t.shape[2]
            pattern = [list(one.ap[0]), [2 * b, P // (2 * b)], [width + b, 2], [1, b]]
            return bass.AP(tensor=one.tensor, offset=one.offset, ap=pattern)

        Q_HALF, K_HALF = (1, 0), (0, 1)

        def total_of(d, i):
            n = ALL >> i
            if i == 0:
                return gates[d][:, :]
            return (totals[d] if i % 2 else totals_even[d])[:, 0:n]

        def add_squares(ops, engine, norm, j):
            m, half = place(norm, j)
            acc = square_acc[half][:, :]
            n = NSQ * norm + j
            if m == 0:
                engine.wait_ge(S["squares_ready"], n + 1)
                ops.tensor_tensor(acc, squares[:, j % 4, :], zero[:, 0:1].broadcast_to([P, HALF]), ALU.add
                                  ).then_inc(S["squares_used"], 1)
            else:
                engine.wait_ge(S["squares_ready"], n + 1)
                engine.wait_ge(S["squares_used"], n)
                ops.tensor_tensor(acc, acc, squares[:, j % 4, :], ALU.add).then_inc(S["squares_used"], 1)

        block = ctx_mgr.enter_context(nc.Block())

        @block.sync
        def _(sp):
            def small_load(dst, src):
                sp.dma_start(dst, src).then_inc(S["small_loaded"], 16)

            def panel(n, slot, src):
                if not (isinstance(n, int) and n < 2):
                    sp.wait_ge(S["panel_split"], n - 1)
                sp.dma_start(w_raw[:, slot, :], src).then_inc(S[f"panel_loaded{slot}"], 16)

            def ada_panel(m, slot):
                if not (isinstance(m, int) and m < 2):
                    sp.wait_ge(S["ada_step"], m * 2 - 2)
                sp.dma_start(ada_raw[:, slot, :], pick(ada, m + ADA_START)).then_inc(S[f"ada_loaded{slot}"], 16)

            small_load(cond_in[:, :], cond)
            small_load(bias[:, :], ada_bias)
            small_load(nw[:, :], norm_w)
            small_load(lbr[:, :], lb_raw)
            small_load(gn[:, :], gnorm)
            small_load(cw[:, :], conv_w)
            def ada_group(g):
                sp.dma_start(ada_first[:, 4 * g:4 * g + 4, :],
                             ada[4 * g:4 * g + 4].rearrange("m p n -> p m n")
                             ).then_inc(S[f"ada_first{g}"], 16)

            ada_group(0)
            for j in range(4):
                if j < 3:
                    ada_group(j + 1)
                m = KB // 4
                sp.dma_start(xt[:, j * m:(j + 1) * m, :],
                             x[j * m:(j + 1) * m].rearrange("k p t -> p k t")).then_inc(S[f"x_loaded{j}"], 16)
            sp.dma_start(ctxt[:, :, :], ctx.rearrange("k p t -> p k t")).then_inc(S["ctx_loaded"], 16)

            def head_loads(h, parity):
                n = N_HEADS + h * HEAD_PANELS
                for i in range(HEAD_PANELS):
                    panel(n + i, (parity + i) % 2, pick(w_hgrn_in, n + i))
                    for a in HEAD_ADA[i]:
                        ada_panel(h * ADA_GROUP + a, a % 2)

            head_loads(0, 0)
            with sp.Fori(0, HEADS // 2 - 1) as i:
                head_loads(i * 2 + 1, 1)
                head_loads(i * 2 + 2, 0)
            head_loads(HEADS - 1, 1)

            def stream(n0, count, src):
                with sp.Fori(0, count // 2) as i:
                    panel(i * 2 + n0, 0, pick(src, i * 2))
                    panel(i * 2 + (n0 + 1), 1, pick(src, i * 2 + 1))

            def hgrn_out_panel(i, slot):
                panel(i + N_HGRN_OUT, slot, pick(w_hgrn_out, i))
                for t in range(2):
                    ada_panel(i * 2 + (ADA_GROUP * G_OUT + t), t)

            hgrn_out_panel(0, 0)
            panel(N_HGRN_OUT + 1, 1, w_hgrn_out[1])
            for t in range(2):
                ada_panel(ADA_GROUP * G_OUT + 2 + t, t)
            hgrn_out_panel(2, 0)
            hgrn_out_panel(3, 1)
            sp.wait_ge(S["mix_ready"], credit["mix_ready"] + 2 * HEADS)
            sp.dma_start(xt[:, :, :], x.rearrange("k p t -> p k t")).then_inc(S["x_reloaded"], 16)
            with sp.Fori(2, KB // 2) as i:
                hgrn_out_panel(i * 2, 0)
                hgrn_out_panel(i * 2 + 1, 1)

            def ffn_loads(n0, w_in, w_out):
                def hidden_panels(n, grp):
                    for j in range(FFN_HIDDEN_PANELS):
                        panel(n + j, j % 2, pick(w_in, grp * 4 + j))

                def out_panels(n, grp):
                    for j in range(FFN_OUT_PANELS):
                        panel(n + j, j % 2, pick(w_out, grp * 2 + j))

                for j in range(FFN_HIDDEN_PANELS):
                    panel(n0 + j, j % 2, w_in[j])
                with sp.Fori(1, FFN_GROUPS) as i:
                    hidden_panels(i * 6 + (n0 - 2), i)
                    out_panels(i * 6 + (n0 + 2), i - 1)
                for j in range(FFN_OUT_PANELS):
                    r = 2 * FFN_GROUPS - 2 + j
                    panel(n0 + 6 * FFN_GROUPS - 2 + j, j % 2, w_out[r])

            ffn_loads(N_FFN0, w_ffn_in[0], w_ffn_out[0])

            with sp.Fori(0, KB // 2) as i:
                for e in range(2):
                    blk = i * 2 + e
                    for j in range(3):
                        panel(blk * 3 + (N_CONV + j), (e + j) % 2, pick(w_conv_in, blk * 3 + j))
                        for a in CONV_ADA[j]:
                            ada_panel(blk * ADA_GROUP + (ADA_GROUP * G_CONV + a), a % 2)
            stream(N_CONV_OUT, KB, w_conv_out)
            ffn_loads(N_FFN1, w_ffn_in[1], w_ffn_out[1])

            for half in range(2):
                for m in range(KB):
                    sp.wait_ge(S["x_updated"], updated(3, m, half))
                    sp.dma_start(out[m][:, cols_of(half)], xt[:, m, cols_of(half)]).then_inc(S["stored"], 16)
            sp.wait_ge(S["stored"], 16 * 2 * KB)

        @block.gpsimd
        def _(pool):
            pool.memset(ones[:, :], 1.0).then_inc(S["consts"], 1)
            pool.memset(zero[:, :], 0.0).then_inc(S["consts"], 1)
            pool.memset(ident[:, :], 0.0).then_inc(S["consts"], 1)
            pool.memset(mask_f32[:, :, :], 1.0).then_inc(S["consts"], 1)
            pool.wait_ge(S["consts"], 4)
            pool.affine_select(out=ident[:, :], in_=ident[:, :], compare_op=ALU.not_equal, fill=1.0,
                               base=0, pattern=[[-1, P]], channel_multiplier=1).then_inc(S["consts"], 1)
            for n, (i, d) in enumerate((i, d) for i in range(LEVELS) for d in (FWD, BWD)):
                b = 1 << i
                m = halves(mask_f32[:, i, :], b)[:, :, Q_HALF[d], :]
                pool.affine_select(out=m, in_=m, compare_op=ALU.is_ge, fill=0.0, base=-b * K_HALF[d],
                                   pattern=[[-2 * b, P // (2 * b)], [0, b]], channel_multiplier=1
                                   ).then_inc(S["masks_f32"], 1)
                pool.wait_ge(S["masks_f32"], 2 * n + 1)
                pool.affine_select(out=m, in_=m, compare_op=ALU.is_ge, fill=0.0,
                                   base=b * K_HALF[d] + b - 1,
                                   pattern=[[2 * b, P // (2 * b)], [0, b]], channel_multiplier=-1
                                   ).then_inc(S["masks_f32"], 1)
            def split(n, slot):
                pool.wait_ge(S[f"panel_loaded{slot}"], (n - slot) * 8 + 16)
                pool.wait_ge(S["panel_started"], n + 1)
                pool.tensor_tensor(w_hi[:, slot, :], w_raw[:, slot, :],
                                   zero[:, 0:1].broadcast_to([P, D]), ALU.add).then_inc(S["w_hi_done"], 1)
                pool.wait_ge(S["w_hi_done"], n + 1)
                pool.tensor_tensor(w_lo[:, slot, :], w_raw[:, slot, :], w_hi[:, slot, :],
                                   ALU.subtract).then_inc(S["panel_split"], 1)

            def splits(n0, n1):
                with pool.Fori(n0 // 2, n1 // 2) as i:
                    for slot in range(2):
                        split(i * 2 + slot, slot)

            def norm_squares(norm):
                for j in range(NSQ):
                    add_squares(pool, pool, norm, j)

            def first_panels(n, norm):
                split(n, 0)
                norm_squares(norm)
                split(n + 1, 1)

            norm_squares(0)
            splits(0, N_HGRN_OUT)
            split(N_HGRN_OUT, 0)
            for half in range(2):
                for m in range(KB - 1):
                    pool.wait_ge(S["mix_hi"], early(half, m) + 1)
                    pool.tensor_tensor(h_lo[:, m, cols_of(half)], mix[:, m, cols_of(half)],
                                       h_hi[:, m, cols_of(half)], ALU.subtract).then_inc(S["mix_split"], 1)
            split(N_HGRN_OUT + 1, 1)
            splits(N_HGRN_OUT + 2, N_FFN0)
            first_panels(N_FFN0, 2)
            splits(N_FFN0 + 2, N_CONV)
            norm_squares(3)
            first_panels(N_CONV, 4)
            splits(N_CONV + 2, N_FFN1)
            first_panels(N_FFN1, 6)
            splits(N_FFN1 + 2, N_PANELS)
            norm_squares(7)

        @block.tensor
        def _(pe):
            def products(out_ap, slot, kb, rhs_hi, rhs_lo, first, last):
                a, b = kb * P, (kb + 1) * P
                pe.matmul(out_ap, w_hi[:, slot, a:b], rhs_hi, start=first, stop=False)
                pe.matmul(out_ap, w_hi[:, slot, a:b], rhs_lo, start=False, stop=False)
                return pe.matmul(out_ap, w_lo[:, slot, a:b], rhs_hi, start=False, stop=last)

            def panel_begin(n):
                pe.wait_ge(S["panel_split"], n + 1)

            def gemm_blocks(n, o, slot, pair, operand_wait=None):
                for half in range(2):
                    dst = bank(2 * pair + half)
                    cols = slice(half * HALF, (half + 1) * HALF)
                    if half == 0:
                        panel_begin(n)
                    pe.wait_ge(S["gemm_evac"], o + half + 1)
                    for kb in range(KB):
                        if operand_wait is not None:
                            operand_wait(half, kb)
                        if half == 0 and kb == 0:
                            pe.matmul(dst, w_hi[:, slot, 0:P], h_hi[:, 0, cols], start=True,
                                      stop=False).then_inc(S["panel_started"], 1)
                            pe.matmul(dst, w_hi[:, slot, 0:P], h_lo[:, 0, cols], start=False, stop=False)
                            mm = pe.matmul(dst, w_lo[:, slot, 0:P], h_hi[:, 0, cols], start=False, stop=False)
                        else:
                            mm = products(dst, slot, kb, h_hi[:, kb, cols], h_lo[:, kb, cols],
                                          kb == 0, kb == KB - 1)
                        if kb == KB - 1:
                            mm.then_inc(S["gemm_full"], 1)
                        yield

            def gemm_panel(n, o, slot, pair, operand_wait=None):
                for _ in gemm_blocks(n, o, slot, pair, operand_wait):
                    pass

            def pair_by_halves(n, o, operand_wait):
                for half in range(2):
                    for slot in range(2):
                        dst = bank(2 * half + slot)
                        if half == 0:
                            panel_begin(n + slot)
                        pe.wait_ge(S["gemm_evac"], o + 2 * half + slot + 1)
                        for kb in range(KB):
                            operand_wait(half, slot, kb)
                            rhs_hi, rhs_lo = h_hi[:, kb, cols_of(half)], h_lo[:, kb, cols_of(half)]
                            if kb == 0 and slot == half:
                                pe.matmul(dst, w_hi[:, slot, 0:P], rhs_hi, start=True,
                                          stop=False).then_inc(S["panel_started"], 1)
                                pe.matmul(dst, w_hi[:, slot, 0:P], rhs_lo, start=False, stop=False)
                                mm = pe.matmul(dst, w_lo[:, slot, 0:P], rhs_hi, start=False, stop=False)
                            else:
                                mm = products(dst, slot, kb, rhs_hi, rhs_lo, kb == 0, kb == KB - 1)
                        mm.then_inc(S["gemm_full"], 1)

            def norm_sums(norm, half):
                pe.wait_ge(S["squares_used"], added(norm, half))
                if half == 1:
                    pe.wait_ge(S["var_done"], 4 * norm + 1)
                for c in range(4):
                    mm = pe.matmul(sum_out[norm][:, 4 * half + c:4 * half + c + 1],
                                   chunk(square_acc[half], c), ones[:, :], start=True, stop=True)
                mm.then_inc(S["summed"], 1)

            def broadcast_rstd(norm, half):
                pe.wait_ge(S["rstd_ready"], 2 * norm + half + 1)
                b = bc(norm, half)
                for c in range(4 * half, 4 * half + 4):
                    mm = pe.matmul(bank(b, (c % 4) * P, (c % 4 + 1) * P), rstd[:, c:c + 1].broadcast_to([P, P]), ident[:, :],
                                   start=True, stop=True)
                mm.then_inc(S["bc_full"], 1)

            def ada_sums(g):
                pe.wait_ge(S["ada_step"], g * 8 + 8)
                if not (isinstance(g, int) and g == 0):
                    pe.wait_ge(S["ada_evac"], g)
                for j in range(ADA_GROUP):
                    mm = pe.matmul(ada_out[:, j:j + 1], ada_acc[:, j * P:(j + 1) * P], ones[:, :],
                                   start=True, stop=True)
                mm.then_inc(S["ada_summed"], 1)

            pe.sem_inc(S["scan_full"], SCAN_USES)
            pe.sem_inc(S["panel_started"], 1)
            pe.sem_inc(S["ada_summed"], 1)
            pe.wait_ge(S["consts"], 5)
            def start_ada(g):
                for cond_of in range(2):
                    pe.wait_ge(S["start_step"], 16 * g + 15 + cond_of)
                    for j in range(ADA_GROUP):
                        c = 2 * (ADA_GROUP * g + j) + cond_of
                        mm = pe.matmul(ada_first_out[:, c:c + 1], start_acc[:, cond_of, g, j * P:(j + 1) * P],
                                       ones[:, :], start=True, stop=True)
                return mm

            for g in range(3):
                start_ada(g)
            norm_sums(0, 0)
            for part in range(2):
                pe.wait_ge(S["csq_ready"], part + 1)
                for j in range(4):
                    for c in range(CCH):
                        mm = pe.matmul(csum_out[:, c:c + 1],
                                       chunk(squares[:, 2 * part + j // 2, :], (j % 2) * CCH + c), ones[:, :],
                                       start=(part == 0 and j == 0 and c == 0), stop=(part == 1 and j == 3),
                                       skip_group_check=True)
                mm.then_inc(S["csq_used"], 1)
            norm_sums(0, 1)
            for half in range(2):
                broadcast_rstd(0, half)
            pe.wait_ge(S["crstd_ready"], 1)
            for c in range(CCH):
                mm = pe.matmul(bank(7, c * P, (c + 1) * P), crstd[:, c:c + 1].broadcast_to([P, P]),
                               ident[:, :], start=True, stop=True)
            mm.then_inc(S["cbc_full"], 1)
            start_ada(3).then_inc(S["ada_first_done"], 1)

            pe.wait_ge(S["cscaled"], 1)

            def scan_use(hh, use):
                earlier = [u for u in range(use) if u % 2 == use % 2]
                if earlier:
                    for name, per_head, idx in scan_readers(earlier[-1]):
                        pe.wait_ge(S[name], hh * per_head + (credit[name] + idx + 1))
                else:
                    before = [u for u in range(SCAN_USES) if u % 2 == use % 2][-1]
                    for name, per_head, idx in scan_readers(before):
                        pe.wait_ge(S[name], hh * per_head + (credit[name] - per_head + idx + 1))
                return SCAN_BANKS[use % 2]

            def transposes(hh, use, src, chunks):
                b = scan_use(hh, use)
                for j, c in enumerate(chunks):
                    mm = pe.transpose(bank(b, j * P, (j + 1) * P), src[:, c * P:(c + 1) * P], ident[:, :])
                mm.then_inc(S["scan_full"], 1)

            def v_transposes(hh, part):
                if part == 0:
                    pe.wait_ge(S["gemm_evac"], hh * 10 + (4 + O_HEADS + 8))
                    pe.wait_ge(S["ctx_evac"], hh * 3 + (1 + 3))
                transposes(hh, U_V + part, v_t, range(4 * part, min(4 * part + 4, CHUNKS)))

            def diagonal(hh, part):
                pe.wait_ge(S["diag_ready"], hh + 1)
                b = scan_use(hh, U_DIAG + part)
                for c in range(4 * part, 4 * part + 4):
                    mm = pe.matmul(bank(b, (c % 4) * P, (c % 4 + 1) * P), chunk(k_sum, c), chunk(q, c),
                                   start=True, stop=True)
                mm.then_inc(S["scan_full"], 1)

            def level(hh, i, part):
                b = scan_use(hh, U_LEVEL + 2 * i + part)
                pe.wait_ge(S["k_merged"], hh * 4 * LEVELS + 2 * (2 * i + part) + 2)
                for d in (FWD, BWD):
                    pe.wait_ge(scan_sem[d], hh * SCAN_STEPS + (1 if i == 0 else 5 * (i - 1) + 3 + 2 * part))
                for c in range(4 * part, 4 * part + 4):
                    mm = pe.matmul(bank(b, (c % 4) * P, (c % 4 + 1) * P), chunk(k_both, c),
                                   both(q_all, c * P, 1 << i), start=True, stop=True)
                mm.then_inc(S["scan_full"], 1)

            def key_transposes(hh, d, part):
                if part == 0:
                    pe.wait_ge(scan_sem[d], hh * SCAN_STEPS + SCAN_STEPS)
                transposes(hh, (U_KF, U_KB)[d] + part, k[d], state_chunks(d)[4 * part:4 * part + 4])

            def key_values(hh, d, part):
                pe.wait_ge(S["scan_evac"], hh * ACT_EVACS + (ACT_EVACS + 3 + 3 * d + part + 1))
                b = scan_use(hh, (U_KVF, U_KVB)[d] + part)
                for j, c in enumerate(state_chunks(d)[4 * part:4 * part + 4]):
                    mm = pe.matmul(bank(b, j * P, (j + 1) * P), k_tok[:, 4 * part + j, :], v_tok[:, c, :],
                                   start=True, stop=True)
                mm.then_inc(S["scan_full"], 1)

            def outputs(hh, part):
                pe.wait_ge(S["scores_evac"], hh * SCORE_EVACS + 2 * SCORE_EVACS)
                for d in (FWD, BWD):
                    pe.wait_ge(state_sem[d], hh * STATE_OPS + 2 * STATE_OPS)
                b = scan_use(hh, U_O + part)
                for c in range(4 * part, 4 * part + 4):
                    dst = bank(b, (c % 4) * P, (c % 4 + 1) * P)
                    pe.matmul(dst, v_tok[:, CCH + c, :], scores[:, c, :], start=True, stop=False)
                    pe.matmul(dst, state[FWD][:, c, :], chunk(qd[FWD], c), start=False, stop=False)
                    mm = pe.matmul(dst, state[BWD][:, c, :], chunk(qd[BWD], c), start=False, stop=True)
                mm.then_inc(S["scan_full"], 1)

            def output_sums(hh):
                pe.wait_ge(S["o_squared"], hh * 2 + (credit["o_squared"] + 2))
                for c in range(LAT):
                    mm = pe.matmul(o_sum_out[:, c:c + 1], chunk(o_sq, c), ones[:, :], start=True, stop=True)
                mm.then_inc(S["o_sum_full"], 1)

            def output_rstd(hh, part):
                pe.wait_ge(S["orstd_ready"], hh + 1)
                b = scan_use(hh, U_BC + part)
                for c in range(4 * part, 4 * part + 4):
                    mm = pe.matmul(bank(b, (c % 4) * P, (c % 4 + 1) * P),
                                   orstd[:, c:c + 1].broadcast_to([P, P]), ident[:, :], start=True, stop=True)
                mm.then_inc(S["scan_full"], 1)

            def out_start():
                for _ in range(16):
                    yield
                for slot in range(2):
                    for half in range(2):
                        dst = bank(2 * half + slot)
                        if half == 0:
                            panel_begin(N_HGRN_OUT + slot)
                        pe.wait_ge(S["gemm_evac"], O_HGRN_OUT + 2 * half + slot + 1)
                        for kb in range(KB - 1):
                            pe.wait_ge(S["mix_split"], early(half, kb) + 1)
                            rhs_hi, rhs_lo = h_hi[:, kb, cols_of(half)], h_lo[:, kb, cols_of(half)]
                            if slot == half == kb == 0:
                                pe.matmul(dst, w_hi[:, 0, 0:P], rhs_hi, start=True,
                                          stop=False).then_inc(S["panel_started"], 1)
                                pe.matmul(dst, w_hi[:, 0, 0:P], rhs_lo, start=False, stop=False)
                                pe.matmul(dst, w_lo[:, 0, 0:P], rhs_hi, start=False, stop=False)
                            else:
                                products(dst, slot, kb, rhs_hi, rhs_lo, kb == 0, False)
                            yield

            def out_start_end():
                a = (KB - 1) * P
                for half in range(2):
                    pe.wait_ge(S["mix_split"], early(half, KB - 1) + 1)
                    rhs_hi, rhs_lo = h_hi[:, KB - 1, cols_of(half)], h_lo[:, KB - 1, cols_of(half)]
                    for slot in range(2):
                        dst = bank(2 * half + slot)
                        mm = pe.matmul(dst, w_hi[:, slot, a:a + P], rhs_hi, start=False, stop=False)
                        if half == slot == 1:
                            mm.then_inc(S["panel_started"], 1)
                        pe.matmul(dst, w_hi[:, slot, a:a + P], rhs_lo, start=False, stop=False)
                        pe.matmul(dst, w_lo[:, slot, a:a + P], rhs_hi, start=False, stop=True
                                  ).then_inc(S["gemm_full"], 1)

            def head(gemm_of, parity, scan_of, first=False):
                hg, hs = gemm_of, scan_of

                def context_block(i, ci):
                    pe.wait_ge(S["ctx_evac"], hg * 3 + (ci + 1))
                    for kb in range(KB):
                        mm = products(ctx_out, (parity + i) % 2, kb, hc_hi[:, kb, :], hc_lo[:, kb, :],
                                      kb == 0, kb == KB - 1)
                    mm.then_inc(S["ctx_full"], 1)

                def steps():
                    if hg is None:
                        yield from out_start()
                        while True:
                            yield
                    for i in range(HEAD_PANELS):
                        wait = (lambda half, kb: pe.wait_ge(S["h_ready"], KB * half + kb + 1)) if first and i == 0 else None
                        n, o = hg * HEAD_PANELS + (N_HEADS + i), hg * 10 + (O_HEADS + 2 * i)
                        yield from gemm_blocks(n, o, (parity + i) % 2, (parity + i) % 2, wait)
                        if i in (0, 1, 3):
                            if first and i == 0:
                                pe.wait_ge(S["hc_ready"], 1)
                            context_block(i, {0: 0, 1: 1, 3: 2}[i])
                    if hs is not None:
                        pe.wait_ge(S["ovar_done"], hs * 2 + 1)
                    ada_sums(hg)

                it = steps()

                def slots(n):
                    for _ in range(n):
                        next(it)

                if hs is not None:
                    slots(7)
                    for part in range(3):
                        v_transposes(hs, part)
                        slots(1)
                    slots(4)
                    diagonal(hs, 0)
                    slots(1)
                    diagonal(hs, 1)
                    slots(1)
                    for i in range(LEVELS):
                        for part in range(2):
                            level(hs, i, part)
                            slots(2 + part)
                    slots(3)
                    for d in (FWD, BWD):
                        for part in range(3):
                            key_transposes(hs, d, part)
                            slots(1)
                        for part in range(3):
                            key_values(hs, d, part)
                            slots(1)
                    slots(4)
                    for part in range(2):
                        outputs(hs, part)
                        slots(1)
                    slots(1)
                    output_sums(hs)
                    slots(5)
                    for part in range(2):
                        output_rstd(hs, part)
                        slots(1)
                if hg is not None:
                    for _ in it:
                        pass

            head(0, 0, None, first=True)
            with pe.Fori(0, HEADS // 2 - 1) as i:
                head(i * 2 + 1, 1, i * 2)
                head(i * 2 + 2, 0, i * 2 + 1)
            head(HEADS - 1, 1, HEADS - 2)
            head(None, 0, HEADS - 1)

            def out_projection(n0, o0, norm, split_before=None, group=None):
                if split_before is None:
                    out_start_end()
                else:
                    pair_by_halves(n0, o0, lambda half, slot, kb: pe.wait_ge(
                        S["mix_split"], split_before + KB * half + kb + 1))
                if group is not None:
                    ada_sums(group)
                with pe.Fori(1, KB // 2 - 1) as i:
                    gemm_panel(i * 2 + n0, i * 4 + o0, 0, 0)
                    gemm_panel(i * 2 + (n0 + 1), i * 4 + (o0 + 2), 1, 1)
                    if group is not None:
                        ada_sums(i + group)
                n, o = n0 + KB - 2, o0 + 2 * KB - 4
                gemm_panel(n, o, 0, 0)
                if group is not None:
                    ada_sums(group + 3)
                for step, _ in enumerate(gemm_blocks(n + 1, o + 2, 1, 1)):
                    if step == KB + 3:
                        norm_sums(norm, 0)
                    if step == KB + 5:
                        broadcast_rstd(norm, 0)
                norm_sums(norm, 1)
                broadcast_rstd(norm, 1)

            def next_norm(norm):
                norm_sums(norm, 0)
                broadcast_rstd(norm, 0)

            def start_wait(norm, before):
                def wait(half, slot, kb):
                    if half == 0 and slot == 0 and kb == 4:
                        norm_sums(norm, 1)
                    if slot == 0:
                        pe.wait_ge(S["h_ready"], before + KB * half + kb + 1)
                    if half == 0 and slot == 1 and kb == 3:
                        broadcast_rstd(norm, 1)
                return wait

            def ffn(f, n0, o0, wait, norm):
                def hidden_panels(n, o, first=0):
                    for j in range(first, FFN_HIDDEN_PANELS):
                        gemm_panel(n + j, o + 2 * j, j % 2, j % 2)

                def out_panels(n, grp, buf):
                    pe.wait_ge(S["hidden_ready"], grp * 4 + (4 * FFN_GROUPS * f + 4))
                    for j in range(FFN_OUT_PANELS):
                        panel_begin(n + j)
                        for m in range(4):
                            for half in range(2):
                                idx = j * 8 + m * 2 + half
                                cols = slice(half * HALF, (half + 1) * HALF)
                                dst = bank(4 + idx % 4)
                                pe.wait_ge(S["partial_evac"], grp * 16 + (16 * FFN_GROUPS * f + idx + 1))
                                for kb in range(2):
                                    a = (kb * 4 + m) * P
                                    mm = pe.matmul(dst, w_hi[:, j, a:a + P], hidden_hi[buf][:, kb, cols],
                                                   start=(kb == 0), stop=False)
                                    if m == 0 and half == 0 and kb == 0:
                                        mm.then_inc(S["panel_started"], 1)
                                    pe.matmul(dst, w_hi[:, j, a:a + P], hidden_lo[buf][:, kb, cols],
                                              start=False, stop=False)
                                    mm = pe.matmul(dst, w_lo[:, j, a:a + P], hidden_hi[buf][:, kb, cols],
                                                   start=False, stop=(kb == 1))
                                mm.then_inc(S["partial_full"], 1)

                def last_out_panels(n, grp, buf):
                    base_f = 16 * FFN_GROUPS * f + 16 * grp
                    pe.wait_ge(S["hidden_ready"], grp * 4 + (4 * FFN_GROUPS * f + 4))
                    for half in range(2):
                        cols = cols_of(half)
                        for j in range(FFN_OUT_PANELS):
                            if half == 0:
                                panel_begin(n + j)
                            for m in range(4):
                                idx = half * 8 + j * 4 + m
                                dst = bank(4 + idx % 4)
                                pe.wait_ge(S["partial_evac"], base_f + idx + 1)
                                for kb in range(2):
                                    a = (kb * 4 + m) * P
                                    mm = pe.matmul(dst, w_hi[:, j, a:a + P], hidden_hi[buf][:, kb, cols],
                                                   start=(kb == 0), stop=False)
                                    if m == 0 and half == j and kb == 0:
                                        mm.then_inc(S["panel_started"], 1)
                                    pe.matmul(dst, w_hi[:, j, a:a + P], hidden_lo[buf][:, kb, cols],
                                              start=False, stop=False)
                                    mm = pe.matmul(dst, w_lo[:, j, a:a + P], hidden_hi[buf][:, kb, cols],
                                                   start=False, stop=(kb == 1))
                                mm.then_inc(S["partial_full"], 1)
                                if idx == KB + 3:
                                    norm_sums(norm, 0)
                    broadcast_rstd(norm, 0)
                    norm_sums(norm, 1)
                    broadcast_rstd(norm, 1)

                pair_by_halves(n0, o0, wait)
                hidden_panels(n0, o0, 2)
                with pe.Fori(0, (FFN_GROUPS - 1) // 2) as i:
                    for e in range(2):
                        hidden_panels(i * 12 + (n0 + 4 + 6 * e), i * 16 + (o0 + 8 + 8 * e))
                        out_panels(i * 12 + (n0 + 8 + 6 * e), i * 2 + e, e)
                last_out_panels(n0 + 6 * FFN_GROUPS - 2, FFN_GROUPS - 1, 0)

            out_projection(N_HGRN_OUT, O_HGRN_OUT, 1, group=G_OUT)
            next_norm(2)
            ffn(0, N_FFN0, O_FFN0, start_wait(2, NSQ), 3)
            next_norm(4)

            def conv_block(blk, e, first=0):
                for j in range(first, 3):
                    gemm_panel(blk * 3 + (N_CONV + j), blk * 6 + (O_CONV + 2 * j), (e + j) % 2, (e + j) % 2)
                ada_sums(blk + G_CONV)

            pair_by_halves(N_CONV, O_CONV, start_wait(4, 2 * NSQ))
            conv_block(0, 0, 2)
            conv_block(1, 1)
            with pe.Fori(1, KB // 2) as i:
                conv_block(i * 2, 0)
                conv_block(i * 2 + 1, 1)
            out_projection(N_CONV_OUT, O_CONV_OUT, 5, NSQ)
            next_norm(6)
            ffn(1, N_FFN1, O_FFN1, start_wait(6, 3 * NSQ), 7)

        @block.scalar
        def _(act):
            def copy(dst, src, sem, func=ACT.Copy, **kw):
                nc.scalar.activation(dst, src, func, **kw).then_inc(S[sem], 1)

            def constants():
                act.wait_ge(S["consts"], 5)

            def square_step(norm, j, t):
                m, half = place(norm, j)
                if NSQ * norm + j >= 4:
                    act.wait_ge(S["squares_used"], NSQ * norm + j - 3)
                copy(squares[:, j % 4, :], t[:, m, cols_of(half)], "squares_ready", ACT.Square)

            def root(norm, half):
                c = slice(4 * half, 4 * half + 4)
                act.wait_ge(S["var_done"], 4 * norm + 2 * half + 2)
                copy(rstd[:, c], inv_var[:, c], "rstd_ready", ACT.Sqrt)

            act.sem_inc(S["gemm_evac"], 4)
            act.sem_inc(S["ctx_evac"], 1)
            for name in ("scan_evac", "o_squared"):
                act.sem_inc(S[name], credit[name])
            act.wait_ge(S["small_loaded"], 16 * 6)
            copy(silu_cond[:, :], cond_in[:, :], "silu_done", ACT.Silu)
            copy(lb_exp[:, 0:KB], lbr[:, :], "params", ACT.Copy)
            act.wait_ge(S["params"], 2)
            copy(lb_exp[:, KB:2 * KB], lb_exp[:, KB:2 * KB], "params", ACT.Exp)
            act.wait_ge(S["gates_done"], 1)
            for j in range(NSQ):
                if j % 4 == 0:
                    act.wait_ge(S[f"x_loaded{j // 4}"], 16)
                square_step(0, j, xt)
            act.wait_ge(S["ctx_loaded"], 16)
            for part in range(2):
                act.wait_ge(S["squares_used"], NSQ - 2 + 2 * part)
                copy(squares[:, 2 * part:2 * part + 2, :].rearrange("p s (k t) -> p (s k) t", t=CTX),
                     ctxt[:, 4 * part:4 * part + 4, :], "csq_ready", ACT.Square)
            root(0, 0)
            root(0, 1)
            act.wait_ge(S["cvar_done"], 2)
            copy(crstd[:, :], cvar[:, CCH:2 * CCH], "crstd_ready", ACT.Sqrt)

            def residual_square(norm, sub, j):
                m, half = place(norm, j)
                act.wait_ge(S["x_updated"], updated(sub, m, half))
                square_step(norm, j, xt)

            def residual_squares(norm, sub):
                for j in range(KB + 4):
                    residual_square(norm, sub, j)
                    if j == KB - 1:
                        root(norm, 0)

            def modulate(norm, inst, scale, shift):
                for half in range(2):
                    for m in range(KB):
                        n = NSQ * inst + KB * half + m
                        act.wait_ge(S["scaled_done"], n + 1)
                        if n >= 4:
                            act.wait_ge(S["h_ready"], n - 3)
                        copy(modulated[:, m % 4, :], scaled[:, m % 4, :], "modulated_done", ACT.Identity,
                             scale=scale[:, m:m + 1], bias=shift[:, m:m + 1])
                        act.wait_ge(S["modulated_done"], n + 1)
                        copy(h_hi[:, m, cols_of(half)], modulated[:, m % 4, :], "h_hi_done")
                        if norm > 0 and half == 0 and m < 4:
                            residual_square(norm, inst - 1, KB + 4 + m)
                        if norm > 0 and half == 0 and m == KB - 1:
                            root(norm, 1)

            act.wait_ge(S["cmod_done"], 4)
            act.wait_ge(S["cscaled"], 1)
            modulate(0, 0, in_scale[:, 0:KB], mods[:, 0:KB])
            for m in range(KB):
                copy(ctxt[:, m, :], ctxt[:, m, :], "cmodulated", ACT.Identity,
                     scale=in_scale[:, 4 * KB + m:4 * KB + m + 1], bias=cmods[:, m:m + 1])
            act.wait_ge(S["cmodulated"], KB)
            copy(hc_hi[:, :, :], ctxt[:, :, :], "chi_done")

            def head(gemm_of, scan_of, parity):
                hg, hs = gemm_of, scan_of

                def evacuate(i, half, dst, **kw):
                    o = hg * 10 + (O_HEADS + 2 * i + half)
                    act.wait_ge(S["gemm_full"], o + 1)
                    copy(dst, bank(2 * ((parity + i) % 2) + half), "gemm_evac", **kw)

                def evacuate_ctx(ci, dst):
                    act.wait_ge(S["ctx_full"], hg * 3 + (ci + 1))
                    copy(dst, ctx_out, "ctx_evac")

                def cols(t, half, off=0):
                    return t[:, off + half * HALF:off + (half + 1) * HALF]

                def scan_bank(use):
                    act.wait_ge(S["scan_full"], hs * SCAN_USES + (SCAN_USES + use + 1))
                    return SCAN_BANKS[use % 2]

                def chunks_out(use, dst, n):
                    b = scan_bank(use)
                    copy(dst, bank(b, 0, n * P).rearrange("p (c t) -> p c t", t=P), "scan_evac")

                def key_tokens(d, part):
                    n = min(4, CHUNKS - 1 - 4 * part)
                    chunks_out((U_KF, U_KB)[d] + part, k_tok[:, 4 * part:4 * part + n, :], n)

                if hs is not None:
                    act.wait_ge(S["gemm_evac"], hs * 10 + (4 + O_HEADS + 4))
                    act.wait_ge(S["ctx_evac"], hs * 3 + 3)
                    act.wait_ge(S["scan_full"], hs * SCAN_USES + SCAN_USES)
                    for d in (FWD, BWD):
                        copy(gates[d][:, :], z[d][:, :], "sigmoids", ACT.Sigmoid)
                        copy(k[d][:, :], z[d][:, :], "sigmoids", ACT.Sigmoid, scale=-1.0)
                    for part in range(3):
                        n = min(4, CHUNKS - 4 * part)
                        chunks_out(U_V + part, v_tok[:, 4 * part:4 * part + n, :], n)
                    act.wait_ge(S["gemm_evac"], hs * 10 + (4 + O_HEADS + 10))
                    constants()
                    copy(mix[:, bass.ds(hs, 1), :], g[:, :].unsqueeze(1), "gate_sig", ACT.Sigmoid)
                    if hg is None:
                        act.wait_ge(S["gemm_full"], O_HGRN_OUT)
                        act.wait_ge(S["mix_ready"], credit["mix_ready"] + 2 * (KB - 1))
                        for half in range(2):
                            for m in range(KB - 1):
                                copy(h_hi[:, m, cols_of(half)], mix[:, m, cols_of(half)], "mix_hi")
                def merge_keys(i, part):
                    if i == 0:
                        act.wait_ge(S["gates_done"], hs * 6 + 7)
                        act.wait_ge(S["scan_full"], hs * SCAN_USES + (SCAN_USES + U_DIAG + 2))
                    else:
                        act.wait_ge(S["scan_full"], hs * SCAN_USES + (SCAN_USES + U_LEVEL + 2 * i - 2 + part + 1))
                    for d in (FWD, BWD):
                        if i > 0:
                            act.wait_ge(scan_sem[d], hs * SCAN_STEPS + (5 * (i - 1) + 2 + 2 * part))
                        src = lat(k[d])[:, part * HALF:(part + 1) * HALF]
                        copy(halves(cols(k_both, part), 1 << i)[:, :, K_HALF[d], :],
                             halves(src, 1 << i)[:, :, K_HALF[d], :], "k_merged")

                def merge_level(i):
                    if hs is not None:
                        for part in range(2):
                            merge_keys(i, part)

                if hg is not None:
                    for half in range(2):
                        evacuate(0, half, cols(z[FWD], half, CTX))
                merge_level(0)
                if hg is not None:
                    evacuate_ctx(0, z[FWD][:, 0:CTX])
                merge_level(1)
                if hg is not None:
                    evacuate(1, 0, cols(z[BWD], 0, CTX))
                merge_level(2)
                if hs is not None:
                    merge_keys(3, 0)
                if hg is not None:
                    evacuate(1, 1, cols(z[BWD], 1, CTX))
                if hs is not None:
                    merge_keys(3, 1)
                if hg is not None:
                    evacuate_ctx(1, z[BWD][:, 0:CTX])
                merge_level(4)
                if hg is not None:
                    if hs is not None:
                        act.wait_ge(S["scan_full"], hs * SCAN_USES + (SCAN_USES + U_DIAG + 2))
                        act.wait_ge(S["scan_b"], hs * SCAN_STEPS + 1)
                    evacuate(2, 0, cols(q, 0), scale=float(P) ** -0.5)
                merge_level(5)
                if hs is not None:
                    merge_keys(6, 0)
                if hg is not None:
                    evacuate(2, 1, cols(q, 1), scale=float(P) ** -0.5)
                if hs is not None:
                    merge_keys(6, 1)
                if hs is not None:
                    for part in range(3):
                        key_tokens(FWD, part)
                    for part in range(3):
                        key_tokens(BWD, part)
                if hg is not None:
                    if hs is not None:
                        act.wait_ge(S["scan_full"], hs * SCAN_USES + (SCAN_USES + U_V + 3))
                    for half in range(2):
                        evacuate(3, half, cols(v_t, half, CTX))
                    evacuate_ctx(2, v_t[:, 0:CTX])
                if hs is not None:
                    for part in range(2):
                        b = scan_bank(U_O + part)
                        copy(cols(o_sq, part), bank(b), "o_squared", ACT.Square)
                    act.wait_ge(S["ovar_done"], hs * 2 + 2)
                    copy(orstd[:, :], ovar[:, LAT:2 * LAT], "orstd_ready", ACT.Sqrt)
                if hg is not None:
                    if hs is not None:
                        act.wait_ge(S["gs_ready"], hs + 1)
                    for half in range(2):
                        evacuate(4, half, cols(g, half))

            act.wait_ge(S["scaled_done"], NSQ)
            head(0, None, 0)
            act.wait_ge(S["hc_ready"], 1)
            with act.Fori(0, HEADS // 2 - 1) as i:
                head(i * 2 + 1, i * 2, 1)
                head(i * 2 + 2, i * 2 + 1, 0)
            head(HEADS - 1, HEADS - 2, 1)
            head(None, HEADS - 1, 0)

            def split_mix(before, ready, last_started):
                act.wait_ge(S["gemm_full"], last_started)
                for half in range(2):
                    for m in range(KB):
                        ready(m, half)
                        copy(h_hi[:, m, cols_of(half)], mix[:, m, cols_of(half)], "mix_hi")

            def out_projection(o0, norm):
                def out_half(m, half, pos):
                    act.wait_ge(S["gemm_full"], o0 + pos + 1)
                    copy(y[:, m, cols_of(half)], bank(pos % 4), "gemm_evac")

                def squares_of(m, half, pos):
                    act.wait_ge(S["gemm_evac"], 4 + o0 + pos + 1)
                    square_step(norm, 2 * m + half, y)

                for pos, (m, half) in enumerate(((0, 0), (1, 0), (0, 1), (1, 1))):
                    out_half(m, half, pos)
                for m, half, pos in ((0, 0, 0), (0, 1, 2), (1, 0, 1), (1, 1, 3)):
                    squares_of(m, half, pos)
                for m in range(2, KB):
                    for half in range(2):
                        out_half(m, half, 2 * m + half)
                        squares_of(m, half, 2 * m + half)
                        if m == KB - 1:
                            root(norm, half)

            def ffn(f, o0, norm):
                def hidden_block(blk, o):
                    for half in range(2):
                        act.wait_ge(S["hidden_done"], blk * 2 + (4 * FFN_GROUPS * f + half + 1))
                        act.wait_ge(S["gemm_full"], o + half + 1)
                        copy(gate_act[:, half, :], bank(half), "gemm_evac", ACT.Silu)
                    for half in range(2):
                        act.wait_ge(S["gemm_full"], o + 2 + half + 1)
                        copy(up_copy[:, half, :], bank(2 + half), "gemm_evac")

                act.wait_ge(S["h_ready"], NSQ * (2 + 2 * f))
                for half in range(2):
                    act.wait_ge(S["hidden_done"], 4 * FFN_GROUPS * f + half + 1)
                    act.wait_ge(S["gemm_full"], o0 + 2 * half + 1)
                    copy(gate_act[:, half, :], bank(2 * half), "gemm_evac", ACT.Silu)
                    act.wait_ge(S["gemm_full"], o0 + 2 * half + 2)
                    copy(up_copy[:, half, :], bank(2 * half + 1), "gemm_evac")
                with act.Fori(1, 2 * FFN_GROUPS) as i:
                    hidden_block(i, i * 4 + o0)
                for j in range(NSQ):
                    act.wait_ge(S["partial_evac"], 4 + 16 * FFN_GROUPS * (f + 1) - 16 + j + 1)
                    square_step(norm, j, y)
                    if j % KB == KB - 1:
                        root(norm, j // KB)

            for half in range(2):
                act.wait_ge(S["mix_ready"], credit["mix_ready"] + 2 * (KB - 1) + half + 1)
                copy(h_hi[:, KB - 1, cols_of(half)], mix[:, KB - 1, cols_of(half)], "mix_hi")
            out_projection(O_HGRN_OUT, 1)
            residual_squares(2, 0)
            act.wait_ge(S["mods_ready"], 2)
            modulate(2, 1, in_scale[:, KB:2 * KB], mods[:, 3 * KB:4 * KB])
            ffn(0, O_FFN0, 3)
            residual_squares(4, 1)
            act.wait_ge(S["mods_ready"], 4)
            modulate(4, 2, in_scale[:, 2 * KB:3 * KB], mods[:, 6 * KB:7 * KB])

            def conv_block(blk, e, first=0):
                for j, (dst, need) in list(enumerate(((conv_c, 1), (conv_x, 1), (conv_b, 5))))[first:]:
                    act.wait_ge(S["conv_done"], blk * 5 + need)
                    for half in range(2):
                        act.wait_ge(S["gemm_full"], blk * 6 + (O_CONV + 2 * j + half + 1))
                        copy(dst[:, half * HALF:(half + 1) * HALF], bank(2 * ((e + j) % 2) + half), "gemm_evac")

            act.wait_ge(S["conv_done"], 1)
            for pos in range(4):
                act.wait_ge(S["gemm_full"], O_CONV + pos + 1)
                copy((conv_c, conv_x)[pos % 2][:, cols_of(pos // 2)], bank(pos), "gemm_evac")
            conv_block(0, 0, 2)
            conv_block(1, 1)
            with act.Fori(1, KB // 2) as i:
                conv_block(i * 2, 0)
                conv_block(i * 2 + 1, 1)
            split_mix(NSQ, lambda m, half: act.wait_ge(S["conv_done"], 5 + 5 * m + 5), O_CONV_OUT)
            out_projection(O_CONV_OUT, 5)
            residual_squares(6, 2)
            act.wait_ge(S["mods_ready"], 6)
            modulate(6, 3, in_scale[:, 3 * KB:4 * KB], mods[:, 9 * KB:10 * KB])
            ffn(1, O_FFN1, 7)

        @block.vector
        def _(dve):
            V = nc.vector

            def tt(dst, a, b, op, sem):
                V.tensor_tensor(dst, a, b, op).then_inc(S[sem], 1)

            for name in ("scores_evac", "state_f", "state_b", "o_gated", "mix_ready"):
                dve.sem_inc(S[name], credit[name])
            dve.sem_inc(S["hidden_done"], 2)
            dve.sem_inc(S["partial_evac"], 4)
            dve.sem_inc(S["conv_done"], 5)

            dve.wait_ge(S["small_loaded"], 16 * 6)
            dve.wait_ge(S["params"], 1)
            one_layer = lb_exp[:, 0:KB]
            e = lb_exp[:, KB:2 * KB]
            inv = lb_exp[:, 2 * KB:3 * KB]
            tt(e, lbr[:, :], one_layer, ALU.subtract, "params")
            dve.wait_ge(S["masks_f32"], 4 * LEVELS)
            V.tensor_copy(masks[:, :, :], mask_f32[:, :, :]).then_inc(S["gates_done"], 1)
            dve.wait_ge(S["params"], 3)
            V.reciprocal(inv, e).then_inc(S["params"], 1)
            dve.wait_ge(S["params"], 4)
            tt(e, e, inv, ALU.mult, "params")
            dve.wait_ge(S["params"], 5)
            tt(lb[:, :], e, e, ALU.subtract, "params")
            dve.wait_ge(S["params"], 6)
            V.tensor_scalar(one_minus_lb[:, :], lb[:, :], -1.0, 1.0, ALU.mult, ALU.add).then_inc(S["params"], 1)
            dve.wait_ge(S["params"], 7)
            dve.wait_ge(S["gates_done"], 1)

            def variance(norm, half):
                c = slice(4 * half, 4 * half + 4)
                dve.wait_ge(S["summed"], 2 * norm + half + 1)
                V.tensor_scalar(var[:, c], sum_out[norm][:, c], 1.0 / D, EPS, ALU.mult, ALU.add
                                ).then_inc(S["var_done"], 1)
                dve.wait_ge(S["var_done"], 4 * norm + 2 * half + 1)
                V.reciprocal(inv_var[:, c], var[:, c]).then_inc(S["var_done"], 1)

            def make_h(norm, inst):
                def low(half, m):
                    dve.wait_ge(S["h_hi_done"], NSQ * inst + KB * half + m + 1)
                    tt(h_lo[:, m, cols_of(half)], modulated[:, m % 4, :], h_hi[:, m, cols_of(half)],
                       ALU.subtract, "h_ready")

                for half in range(2):
                    dve.wait_ge(S["bc_full"], 2 * norm + half + 1)
                    for m in range(KB):
                        n = NSQ * inst + KB * half + m
                        if n >= 4:
                            dve.wait_ge(S["modulated_done"], n - 3)
                        tt(scaled[:, m % 4, :], xt[:, m, cols_of(half)], bank(bc(norm, half)), ALU.mult, "scaled_done")
                        if m >= 2:
                            low(half, m - 2)
                    low(half, KB - 2)
                    low(half, KB - 1)
                    if norm > 0 and half == 0:
                        variance(norm, 1)

            def add_residual(norm, sub):
                for half in range(2):
                    if norm in BY_BLOCK and half == 0:
                        add_squares(V, dve, norm, NSQ - 1)
                    dve.wait_ge(S["bc_full"], 2 * norm + half + 1)
                    n0 = 2 * KB * (2 * sub + half)
                    cols = cols_of(half)
                    for m in range(KB + 1):
                        if m < KB:
                            tt(y[:, m, cols], y[:, m, cols], bank(bc(norm, half)), ALU.mult, "x_updated")
                        if m == 0:
                            continue
                        r = m - 1
                        dve.wait_ge(S["x_updated"], n0 + (2 * r + 1 if r == 0 else 2 * r))
                        V.scalar_tensor_tensor(xt[:, r, cols], y[:, r, cols],
                                               out_scale[:, sub * KB + r:sub * KB + r + 1],
                                               xt[:, r, cols], ALU.mult, ALU.add).then_inc(S["x_updated"], 1)
                        if m == 2 and half == 0:
                            variance(norm, 1)
                        if m == 6 and half == 1 and norm < 7:
                            variance(norm + 1, 0)

            dve.wait_ge(S["silu_done"], 1)
            for g_first in range(ADA_START // ADA_GROUP):
                dve.wait_ge(S[f"ada_first{g_first}"], 16)
                for kb in range(KB):
                    src = ada_first[:, ADA_GROUP * g_first + kb // 2, (kb % 2) * HALF:(kb % 2 + 1) * HALF]
                    for cond_of in range(2):
                        acc = start_acc[:, cond_of, g_first, :]
                        weight = silu_cond[:, 2 * kb + cond_of:2 * kb + cond_of + 1]
                        if kb == 0:
                            V.tensor_scalar(acc, src, weight, None, ALU.mult).then_inc(S["start_step"], 1)
                        else:
                            dve.wait_ge(S["start_step"], 16 * g_first + 2 * kb + cond_of - 1)
                            V.scalar_tensor_tensor(acc, src, weight, acc, ALU.mult, ALU.add
                                                   ).then_inc(S["start_step"], 1)
            variance(0, 0)
            variance(0, 1)
            dve.wait_ge(S["csq_used"], 2)
            V.tensor_scalar(cvar[:, 0:CCH], csum_out, 1.0 / D, EPS, ALU.mult, ALU.add).then_inc(S["cvar_done"], 1)
            dve.wait_ge(S["cvar_done"], 1)
            V.reciprocal(cvar[:, CCH:2 * CCH], cvar[:, 0:CCH]).then_inc(S["cvar_done"], 1)
            dve.wait_ge(S["cbc_full"], 1)
            tt(ctxt[:, :, :], ctxt[:, :, :], bank(7, 0, CTX).unsqueeze(1).broadcast_to([P, KB, CTX]),
               ALU.mult, "cscaled")
            dve.wait_ge(S["ada_first_done"], 1)
            sums = ada_first_out.rearrange("p (m two) -> p two m", two=2)
            tt(mods[:, 0:2 * KB], sums[:, 0, :], bias[:, 0:2 * KB], ALU.add, "cmod_done")
            tt(cmods[:, :], sums[:, 1, :], bias[:, 0:2 * KB], ALU.add, "cmod_done")
            dve.wait_ge(S["cmod_done"], 2)

            def weigh(dst, scale, weights, sem):
                V.scalar_tensor_tensor(dst, scale, 1.0, weights, ALU.add, ALU.mult).then_inc(S[sem], 1)

            weigh(in_scale[:, 0:KB], mods[:, KB:2 * KB], nw[:, 0:KB], "cmod_done")
            weigh(in_scale[:, 4 * KB:5 * KB], cmods[:, KB:2 * KB], nw[:, 0:KB], "cmod_done")
            make_h(0, 0)
            dve.wait_ge(S["chi_done"], 1)
            tt(hc_lo[:, :, :], ctxt[:, :, :], hc_hi[:, :, :], ALU.subtract, "hc_ready")

            def ada_rows(g, a):
                dve.wait_ge(S[f"ada_loaded{a % 2}"], g * 32 + 16 * (a // 2 + 1))
                for t in range(2):
                    kb = 2 * a + t
                    src = ada_raw[:, a % 2, t * HALF:(t + 1) * HALF]
                    weight = silu_cond[:, 2 * kb:2 * kb + 1]
                    if kb == 0:
                        dve.wait_ge(S["ada_summed"], g + 1)
                        V.tensor_scalar(ada_acc[:, :], src, weight, None, ALU.mult).then_inc(S["ada_step"], 1)
                    else:
                        dve.wait_ge(S["ada_step"], g * 8 + kb)
                        V.scalar_tensor_tensor(ada_acc[:, :], src, weight, ada_acc[:, :],
                                               ALU.mult, ALU.add).then_inc(S["ada_step"], 1)

            def ada_bias_add(g):
                dve.wait_ge(S["ada_summed"], g + 2)
                cols = bass.ds(g * ADA_GROUP + ADA_START, ADA_GROUP)
                tt(mods[:, cols], ada_out, bias[:, cols], ALU.add, "ada_evac")

            def head(gemm_of, scan_of):
                hg, hs = gemm_of, scan_of

                def scan_bank(use):
                    dve.wait_ge(S["scan_full"], hs * SCAN_USES + (SCAN_USES + use + 1))
                    return SCAN_BANKS[use % 2]

                def q_and_totals(d):
                    V.tensor_tensor(qd[d][:, :], q[:, :], lat(gates[d]), ALU.mult).then_inc(scan_sem[d], 1)

                def decay_level(i):
                    b = 1 << i
                    tot = [total_of(d, i).rearrange("p (n two) -> p n two", two=2) for d in (FWD, BWD)]
                    for part in range(2):
                        use = scan_bank(U_LEVEL + 2 * i + part)
                        k0, k1 = (0, CTX + HALF) if part == 0 else (CTX + HALF, ALL)
                        q0, q1 = part * HALF, (part + 1) * HALF
                        for d in (FWD, BWD):
                            if part == 0:
                                dve.wait_ge(scan_sem[d], hs * SCAN_STEPS + (1 + 5 * i))
                            n0, n1 = k0 // (2 * b), k1 // (2 * b)
                            kk = halves(k[d][:, k0:k1], b)[:, :, K_HALF[d], :]
                            V.tensor_tensor(kk, kk, tot[d][:, n0:n1, 1 - K_HALF[d]:2 - K_HALF[d]].broadcast_to(
                                [P, n1 - n0, b]), ALU.mult).then_inc(scan_sem[d], 1)
                            if d == BWD:
                                dve.wait_ge(S["scores_evac"], hs * SCORE_EVACS + (SCORE_EVACS + 2 * i + part + 1))
                            n0, n1 = (CTX + q0) // (2 * b), (CTX + q1) // (2 * b)
                            qq = halves(qd[d][:, q0:q1], b)[:, :, Q_HALF[d], :]
                            V.tensor_tensor(qq, qq, tot[d][:, n0:n1, 1 - Q_HALF[d]:2 - Q_HALF[d]].broadcast_to(
                                [P, n1 - n0, b]), ALU.mult).then_inc(scan_sem[d], 1)
                        V.copy_predicated(scores[:, 4 * part:4 * part + 4, :],
                                          masks[:, i, :].unsqueeze(1).broadcast_to([P, 4, P]),
                                          bank(use).rearrange("p (c t) -> p c t", t=P)
                                          ).then_inc(S["scores_evac"], 1)
                    for d in (FWD, BWD):
                        V.tensor_tensor(total_of(d, i + 1), tot[d][:, :, 0], tot[d][:, :, 1], ALU.mult
                                        ).then_inc(scan_sem[d], 1)

                def states(d, part):
                    order = state_chunks(d)
                    for j in range(4 * part, min(4 * part + 4, CHUNKS - 1)):
                        if j % 4 == 0:
                            use = scan_bank((U_KVF, U_KVB)[d] + part)
                        src = bank(use, (j % 4) * P, (j % 4 + 1) * P)
                        step = -1 if d == BWD else 1
                        first = 0 if d == FWD else LAT - 1

                        def place(s):
                            return state[d][:, first + step * (1 if s == 1 else s - 2), :]

                        if j == 0:
                            dve.wait_ge(scan_sem[d], hs * SCAN_STEPS + SCAN_STEPS)
                            V.tensor_copy(place(1), src).then_inc(state_sem[d], 1)
                        else:
                            dve.wait_ge(state_sem[d], hs * STATE_OPS + (STATE_OPS + j))
                            c = order[j]
                            V.scalar_tensor_tensor(place(j + 1), place(j), total_of(d, LEVELS)[:, c:c + 1], src,
                                                   ALU.mult, ALU.add).then_inc(state_sem[d], 1)

                if hs is not None:
                    lbs, oml = lb[:, bass.ds(hs, 1)], one_minus_lb[:, bass.ds(hs, 1)]
                    base_g = hs * 6 + 1
                    for d in (FWD, BWD):
                        dve.wait_ge(S["sigmoids"], hs * 4 + (2 * d + 1))
                        V.tensor_scalar(gates[d][:, :], gates[d][:, :], oml, lbs, ALU.mult, ALU.add
                                        ).then_inc(S["gates_done"], 1)
                        dve.wait_ge(S["sigmoids"], hs * 4 + (2 * d + 2))
                        V.tensor_scalar(k[d][:, :], k[d][:, :], oml, None, ALU.mult).then_inc(S["gates_done"], 1)
                        dve.wait_ge(S["gates_done"], base_g + (3 * d + 1))
                        V.tensor_scalar(gates[d][:, :], gates[d][:, :], F_FLOOR, None, ALU.max
                                        ).then_inc(S["gates_done"], 1)
                    dve.wait_ge(S["gates_done"], base_g + 6)
                    tt(k_sum[:, :], lat(k[FWD]), lat(k[BWD]), ALU.add, "diag_ready")
                    q_and_totals(FWD)
                    q_and_totals(BWD)
                    own = mix[:, bass.ds(hs, 1), :]
                    dve.wait_ge(S["gate_sig"], hs + 1)
                    tt(own, own, g[:, :].unsqueeze(1), ALU.mult, "gs_ready")
                    for part in range(2):
                        use = scan_bank(U_DIAG + part)
                        tt(scores[:, 4 * part:4 * part + 4, :], bank(use).rearrange("p (c t) -> p c t", t=P),
                           ident[:, :].unsqueeze(1).broadcast_to([P, 4, P]), ALU.mult, "scores_evac")
                    for i in range(LEVELS):
                        decay_level(i)
                        if hg is not None and i == 3:
                            for a in range(2):
                                ada_rows(hg, a)
                    for d in (FWD, BWD):
                        for part in range(3):
                            states(d, part)
                    if hg is not None:
                        for a in range(2, ADA_GROUP):
                            ada_rows(hg, a)
                    dve.wait_ge(S["gs_ready"], hs + 1)
                    for part in range(2):
                        use = scan_bank(U_O + part)
                        half = own[:, :, part * HALF:(part + 1) * HALF]
                        dve.wait_ge(S["o_squared"], hs * 2 + (credit["o_squared"] + part + 1))
                        tt(half, bank(use).unsqueeze(1), half, ALU.mult, "o_gated")
                    dve.wait_ge(S["o_sum_full"], hs + 1)
                    V.tensor_scalar(ovar[:, 0:LAT], o_sum_out, 1.0 / P, EPS, ALU.mult, ALU.add
                                    ).then_inc(S["ovar_done"], 1)
                    dve.wait_ge(S["ovar_done"], hs * 2 + 1)
                    V.reciprocal(ovar[:, LAT:2 * LAT], ovar[:, 0:LAT]).then_inc(S["ovar_done"], 1)
                    for part in range(2):
                        use = scan_bank(U_BC + part)
                        half = own[:, :, part * HALF:(part + 1) * HALF]
                        V.scalar_tensor_tensor(half, half, gn[:, 0:1], bank(use).unsqueeze(1), ALU.mult, ALU.mult
                                               ).then_inc(S["mix_ready"], 1)
                elif hg is not None:
                    for a in range(ADA_GROUP):
                        ada_rows(hg, a)
                if hg is not None:
                    ada_bias_add(hg)

            dve.wait_ge(S["silu_done"], 1)
            head(0, None)
            with dve.Fori(0, HEADS // 2 - 1) as i:
                head(i * 2 + 1, i * 2)
                head(i * 2 + 2, i * 2 + 1)
            head(HEADS - 1, HEADS - 2)
            head(None, HEADS - 1)

            dve.wait_ge(S["ada_evac"], HEADS)
            tt(out_scale[:, 0:KB], mods[:, 2 * KB:3 * KB], nw[:, KB:2 * KB], ALU.mult, "mods_ready")
            weigh(in_scale[:, KB:2 * KB], mods[:, 4 * KB:5 * KB], nw[:, 2 * KB:3 * KB], "mods_ready")
            tt(out_scale[:, KB:2 * KB], mods[:, 5 * KB:6 * KB], nw[:, 3 * KB:4 * KB], ALU.mult, "mods_ready")

            def split_mix(inst):
                for half in range(2):
                    for m in range(KB):
                        dve.wait_ge(S["mix_hi"], NSQ * inst + KB * half + m + 1)
                        tt(h_lo[:, m, cols_of(half)], mix[:, m, cols_of(half)], h_hi[:, m, cols_of(half)],
                           ALU.subtract, "mix_split")

            def ffn(f):
                V.memset(y[:, :, :], 0.0).then_inc(S["y_zeroed"], 1)

                def hidden_block(blk, o, buf, kb, by_halves=False):
                    for half in range(2):
                        cols = slice(half * HALF, (half + 1) * HALF)
                        done = blk * 2 + (4 * FFN_GROUPS * f + half)
                        dve.wait_ge(S["gemm_evac"], o + (4 + (2 * half + 2 if by_halves else half + 3)))
                        tt(hidden[:, half, :], gate_act[:, half, :], up_copy[:, half, :], ALU.mult, "hidden_done")
                        dve.wait_ge(S["hidden_done"], done + 3)
                        V.tensor_copy(hidden_hi[buf][:, kb, cols], hidden[:, half, :]
                                      ).then_inc(S["hidden_hi_done"], 1)
                        dve.wait_ge(S["hidden_hi_done"], done + 1)
                        tt(hidden_lo[buf][:, kb, cols], hidden[:, half, :], hidden_hi[buf][:, kb, cols],
                           ALU.subtract, "hidden_ready")

                def add_last_partials(norm):
                    g0 = 16 * FFN_GROUPS * f + 16 * (FFN_GROUPS - 1)
                    dve.wait_ge(S["partial_evac"], g0 + 4)
                    for idx in range(NSQ):
                        m, half = idx % KB, idx // KB
                        dve.wait_ge(S["partial_full"], g0 + idx + 1)
                        tt(y[:, m, cols_of(half)], y[:, m, cols_of(half)], bank(4 + idx % 4), ALU.add,
                           "partial_evac")
                        if idx == KB + 3:
                            variance(norm, 0)

                def add_partials(grp):
                    g0 = 16 * FFN_GROUPS * f
                    dve.wait_ge(S["partial_evac"], grp * 16 + (g0 + 4))
                    for m in range(KB):
                        for half in range(2):
                            idx = 2 * m + half
                            dst = y[:, m, half * HALF:(half + 1) * HALF]
                            dve.wait_ge(S["partial_full"], grp * 16 + (g0 + idx + 1))
                            tt(dst, dst, bank(4 + idx % 4), ALU.add, "partial_evac")

                def hidden_group(grp, o, buf, first=False):
                    for kb in range(2):
                        hidden_block(grp * 2 + kb, o + 4 * kb, buf, kb, first and kb == 0)

                o0 = (O_FFN0, O_FFN1)[f]
                hidden_group(0, o0, 0, first=True)
                dve.wait_ge(S["y_zeroed"], f + 1)
                with dve.Fori(0, (FFN_GROUPS - 1) // 2) as i:
                    for e in range(2):
                        hidden_group(i * 2 + (e + 1), i * 16 + (o0 + 8 + 8 * e), 1 - e)
                        add_partials(i * 2 + e)
                add_last_partials(AFTER_FFN[f])

            dve.wait_ge(S["mix_split"], early(0, KB - 1))
            for half in range(2):
                dve.wait_ge(S["mix_hi"], early(half, KB - 1) + 1)
                tt(h_lo[:, KB - 1, cols_of(half)], mix[:, KB - 1, cols_of(half)],
                   h_hi[:, KB - 1, cols_of(half)], ALU.subtract, "mix_split")
            for group in range(G_OUT, G_CONV):
                for a in range(ADA_GROUP):
                    ada_rows(group, a)
                if group < G_CONV - 1:
                    for j in range(4 * (group - G_OUT), 4 * (group - G_OUT) + 4):
                        add_squares(V, dve, 1, j)
                ada_bias_add(group)
            for j in range(NSQ - 4, NSQ - 1):
                add_squares(V, dve, 1, j)
            dve.wait_ge(S["ada_evac"], G_CONV)
            weigh(in_scale[:, 2 * KB:3 * KB], mods[:, 7 * KB:8 * KB], nw[:, 4 * KB:5 * KB], "mods_ready")
            variance(1, 0)
            dve.wait_ge(S["x_reloaded"], 16)
            dve.wait_ge(S["mods_ready"], 4)
            add_residual(1, 0)
            make_h(2, 1)
            ffn(0)
            add_residual(3, 1)
            make_h(4, 2)

            def conv_block(blk):
                rows = SEQ // GRID_W
                u = conv_u[:, :].rearrange("p (r w) -> p r w", w=GRID_W)
                v = conv_v[:, :].rearrange("p (r w) -> p r w", w=GRID_W)
                own = mix[:, bass.ds(blk, 1), :]

                def tap(j):
                    return cw[:, bass.ds(blk + j * KB, 1)]

                for a in range(ADA_GROUP):
                    ada_rows(blk + G_CONV, a)
                c0 = blk * 5 + 5
                dve.wait_ge(S["gemm_evac"], blk * 6 + (4 + O_CONV + 4))
                tt(conv_u[:, :], conv_c[:, :], conv_x[:, :], ALU.mult, "conv_done")
                dve.wait_ge(S["conv_done"], c0 + 1)
                V.tensor_scalar(conv_v[:, :], conv_u[:, :], tap(1), None, ALU.mult).then_inc(S["conv_done"], 1)
                dve.wait_ge(S["conv_done"], c0 + 2)
                V.scalar_tensor_tensor(v[:, :, 1:], u[:, :, :GRID_W - 1], tap(0), v[:, :, 1:],
                                       ALU.mult, ALU.add).then_inc(S["conv_done"], 1)
                dve.wait_ge(S["conv_done"], c0 + 3)
                V.scalar_tensor_tensor(v[:, :, :GRID_W - 1], u[:, :, 1:], tap(2), v[:, :, :GRID_W - 1],
                                       ALU.mult, ALU.add).then_inc(S["conv_done"], 1)
                dve.wait_ge(S["gemm_evac"], blk * 6 + (4 + O_CONV + 6))
                dve.wait_ge(S["conv_done"], c0 + 4)
                tt(own, conv_v[:, :].unsqueeze(1), conv_b[:, :].unsqueeze(1), ALU.mult, "conv_done")
                ada_bias_add(blk + G_CONV)

            with dve.Fori(0, KB) as i:
                conv_block(i)
            dve.wait_ge(S["ada_evac"], G_CONV + KB)
            tt(out_scale[:, 2 * KB:3 * KB], mods[:, 8 * KB:9 * KB], nw[:, 5 * KB:6 * KB], ALU.mult, "mods_ready")
            weigh(in_scale[:, 3 * KB:4 * KB], mods[:, 10 * KB:11 * KB], nw[:, 6 * KB:7 * KB], "mods_ready")
            tt(out_scale[:, 3 * KB:4 * KB], mods[:, 11 * KB:12 * KB], nw[:, 7 * KB:8 * KB], ALU.mult, "mods_ready")
            split_mix(1)
            for j in range(NSQ - 1):
                add_squares(V, dve, 5, j)
            variance(5, 0)
            dve.wait_ge(S["mods_ready"], 7)
            add_residual(5, 2)
            make_h(6, 3)
            ffn(1)
            add_residual(7, 3)


def kernel(x, c, ctx, c_ctx, ada_w, ada_b, norm_w, hgrn_w_in, hgrn_w_out, hgrn_gnorm, hgrn_lb,
           conv_w_in, conv_w, conv_w_out, ffn_w_in, ffn_w_out):
    import numpy as np
    import concourse.bacc as bacc
    from concourse.bass_utils import run_bass_kernel_spmd

    a = np.asarray

    def panels(w, parts=1):
        kb, m = w.shape[0] // P, w.shape[1] // parts // P
        return w.reshape(kb, P, parts, m, P).transpose(3, 2, 1, 0, 4)

    def channels(v):
        return a(v).reshape(-1, KB, P).transpose(2, 0, 1).reshape(P, -1)

    arrays = {}
    arrays["x"] = a(x)[0].T.reshape(KB, P, SEQ)
    arrays["ctx"] = a(ctx)[0].T.reshape(KB, P, CTX)
    arrays["cond"] = np.stack([a(c)[0], a(c_ctx)]).reshape(2, KB, P).transpose(2, 1, 0).reshape(P, 2 * KB)
    arrays["ada"] = np.concatenate([w.reshape(ADA_GROUP, 2, P, -1, HALF).transpose(3, 0, 2, 1, 4).reshape(-1, P, D)
                                    for w in a(ada_w)])
    arrays["ada_bias"] = channels(ada_b)
    arrays["norm_w"] = channels(norm_w)
    arrays["lb_raw"] = channels(hgrn_lb)
    arrays["gnorm"] = a(hgrn_gnorm).reshape(P, 1)
    arrays["conv_w"] = channels(conv_w)
    arrays["w_hgrn_in"] = panels(a(hgrn_w_in)[0], 5)[:, list(HEAD_PARTS)].reshape(-1, P, D)
    arrays["w_hgrn_out"] = panels(a(hgrn_w_out)[0]).reshape(-1, P, D)
    arrays["w_conv_in"] = panels(a(conv_w_in)[0], 3)[:, [1, 2, 0]].reshape(-1, P, D)
    arrays["w_conv_out"] = panels(a(conv_w_out)[0]).reshape(-1, P, D)
    arrays["w_ffn_in"] = np.stack([panels(w, 2).reshape(-1, P, D) for w in a(ffn_w_in)])
    arrays["w_ffn_out"] = a(ffn_w_out).reshape(2, FFN_GROUPS, 2, P, 2, 4, P).transpose(
        0, 1, 4, 3, 2, 5, 6).reshape(2, 2 * FFN_GROUPS, P, D)
    arrays = {n: np.ascontiguousarray(v) for n, v in arrays.items()}

    nc = bacc.Bacc("TRN2", target_bir_lowering=False, num_devices=1, dynamic_dma_scratch_size=1024)
    aps = {n: nc.dram_tensor("in_" + n, v.shape, mybir.dt.from_np(v.dtype), kind="ExternalInput").ap()
           for n, v in arrays.items()}
    out = nc.dram_tensor("out", (KB, P, SEQ), F32, kind="ExternalOutput").ap()
    build_trunk(nc, out=out, **aps)
    r = run_bass_kernel_spmd(nc, [{"in_" + n: v for n, v in arrays.items()}], core_ids=[0])
    return r.results[0]["out"].reshape(D, SEQ).T.reshape(1, SEQ, D)
```
